# Optimizing a Trainium2 kernel written in Bass

```python
import math
import jax, jax.numpy as jnp
from jax import lax
import numpy as np

D_MODEL = 1024
BATCH = 1
SEQ = 512
DEPTH = 2

CHUNK = 64
Q_BLOCK = 128
N_A_LAYERS = DEPTH // 2
N_B_LAYERS = DEPTH - N_A_LAYERS
A_HEADS = 8
A_HEAD_DIM = D_MODEL // (2 * A_HEADS)
B_HEADS = 16
B_HEAD_DIM = D_MODEL // B_HEADS
LEFT_CHUNKS = 8
BAND_CHUNKS = LEFT_CHUNKS + 1
MAX_REL_DIST = 256
D_FF = -(-8 * D_MODEL // (3 * 256)) * 256
ROPE_THETA = 10000.0
LN_EPS = 1e-5
SUBLN_EPS = 1e-5
DEEPNORM_ALPHA = (2 * DEPTH) ** 0.25
DEEPNORM_BETA = (8 * DEPTH) ** -0.25


def layer_norm(x, g, b):
    xf = x.astype(jnp.float32)
    mu = jnp.mean(xf, axis=-1, keepdims=True)
    var = jnp.mean(jnp.square(xf - mu), axis=-1, keepdims=True)
    y = (xf - mu) * lax.rsqrt(var + LN_EPS) * g.astype(jnp.float32) + b.astype(jnp.float32)
    return y.astype(x.dtype)

def rms_norm(x, g):
    xf = x.astype(jnp.float32)
    y = xf * lax.rsqrt(jnp.mean(jnp.square(xf), axis=-1, keepdims=True) + SUBLN_EPS)
    return (y * g.astype(jnp.float32)).astype(x.dtype)

def rope_tables(seq, dim):
    inv = ROPE_THETA ** (-jnp.arange(0, dim, 2, dtype=jnp.float32) / dim)
    ang = jnp.arange(seq, dtype=jnp.float32)[:, None] * inv[None, :]
    return jnp.cos(ang), jnp.sin(ang)

def apply_rope(x, cos, sin):
    half = x.shape[-1] // 2
    x1, x2 = x[..., :half], x[..., half:]
    cos = cos.astype(x.dtype)
    sin = sin.astype(x.dtype)
    return jnp.concatenate([x1 * cos - x2 * sin, x1 * sin + x2 * cos], axis=-1)

def lambda_init_fn(layer_idx):
    return 0.8 - 0.6 * math.exp(-0.3 * layer_idx)

def diff_attention(x, w_qkv, lam_params, subln_g, w_o, lambda_init):
    b, s, _ = x.shape
    qkv = x @ w_qkv
    q, k, v = jnp.split(qkv, 3, axis=-1)
    q = q.reshape(b, s, A_HEADS, 2, A_HEAD_DIM)
    k = k.reshape(b, s, A_HEADS, 2, A_HEAD_DIM)
    v = v.reshape(b, s, A_HEADS, 2 * A_HEAD_DIM)
    cos, sin = rope_tables(s, A_HEAD_DIM)
    cos = cos[:, None, None, :]
    sin = sin[:, None, None, :]
    q = apply_rope(q, cos, sin) * (A_HEAD_DIM ** -0.5)
    k = apply_rope(k, cos, sin)
    lp = lam_params.astype(jnp.float32)
    lam = jnp.exp(jnp.sum(lp[0] * lp[1])) - jnp.exp(jnp.sum(lp[2] * lp[3])) + lambda_init
    chunk_id = jnp.arange(s) // CHUNK
    neg = jnp.finfo(jnp.float32).min
    outs = []
    for i in range(s // Q_BLOCK):
        q0 = i * Q_BLOCK
        kend = q0 + Q_BLOCK
        sc = jnp.einsum('bqhmd,bkhmd->bhmqk', q[:, q0:kend], k[:, :kend],
                        preferred_element_type=jnp.float32)
        allowed = chunk_id[None, :kend] <= chunk_id[q0:kend, None]
        p = jax.nn.softmax(jnp.where(allowed, sc, neg), axis=-1)
        a = p[:, :, 0] - lam * p[:, :, 1]
        outs.append(jnp.einsum('bhqk,bkhe->bqhe', a.astype(v.dtype), v[:, :kend]))
    o = jnp.concatenate(outs, axis=1)
    o = rms_norm(o, subln_g) * (1.0 - lambda_init)
    return o.reshape(b, s, D_MODEL) @ w_o

def shared_kv_band(x, kv_w):
    b, s, _ = x.shape
    nc = s // CHUNK
    kv = x @ kv_w
    k, v = jnp.split(kv, 2, axis=-1)
    k = k.reshape(b, nc, CHUNK, B_HEADS, B_HEAD_DIM)
    v = v.reshape(b, nc, CHUNK, B_HEADS, B_HEAD_DIM)
    pad = ((0, 0), (LEFT_CHUNKS, 0), (0, 0), (0, 0), (0, 0))
    kp = jnp.pad(k, pad)
    vp = jnp.pad(v, pad)
    k_band = jnp.concatenate([kp[:, j:j + nc] for j in range(BAND_CHUNKS)], axis=2)
    v_band = jnp.concatenate([vp[:, j:j + nc] for j in range(BAND_CHUNKS)], axis=2)
    band_chunk = jnp.arange(BAND_CHUNKS * CHUNK) // CHUNK
    band_valid = (jnp.arange(nc)[:, None] - LEFT_CHUNKS + band_chunk[None, :]) >= 0
    return k_band, v_band, band_valid

def chunk_attention(x, k_band, v_band, band_valid, w_q, rel_table, w_o):
    b, s, _ = x.shape
    nc = s // CHUNK
    q = (x @ w_q).reshape(b, nc, CHUNK, B_HEADS, B_HEAD_DIM) * (B_HEAD_DIM ** -0.5)
    rel = (jnp.arange(BAND_CHUNKS * CHUNK)[None, :] - LEFT_CHUNKS * CHUNK
           - jnp.arange(CHUNK)[:, None])
    idx = jnp.clip(rel, -MAX_REL_DIST, MAX_REL_DIST) + MAX_REL_DIST
    bias = rel_table[:, idx].astype(jnp.float32)
    sc = jnp.einsum('bnqhd,bnkhd->bhnqk', q, k_band,
                    preferred_element_type=jnp.float32) + bias[:, None]
    sc = jnp.where(band_valid[:, None, :], sc, jnp.finfo(jnp.float32).min)
    p = jax.nn.softmax(sc, axis=-1)
    o = jnp.einsum('bhnqk,bnkhd->bnqhd', p.astype(v_band.dtype), v_band)
    return o.reshape(b, s, D_MODEL) @ w_o

def swiglu(x, w_in, w_out):
    gate, up = jnp.split(x @ w_in, 2, axis=-1)
    return (jax.nn.silu(gate) * up) @ w_out

def first_inputs(seed: int = 0) -> dict:
    key = jax.random.key(seed)
    ks = jax.random.split(key, 14)
    f32 = jnp.float32
    d = D_MODEL
    nrm = lambda k, shape, sc: jax.random.normal(k, shape, f32) * sc
    return {
        "x": nrm(ks[0], (BATCH, SEQ, d), 1.0),
        "a_w_qkv": nrm(ks[1], (N_A_LAYERS, d, 3 * d), d ** -0.5),
        "a_lambda": nrm(ks[2], (N_A_LAYERS, 4, A_HEAD_DIM), 0.1),
        "a_subln_g": 1.0 + nrm(ks[3], (N_A_LAYERS, 2 * A_HEAD_DIM), 0.02),
        "a_w_o": nrm(ks[4], (N_A_LAYERS, d, d), d ** -0.5 * DEEPNORM_BETA),
        "kv_w": nrm(ks[5], (d, 2 * d), d ** -0.5),
        "b_w_q": nrm(ks[6], (N_B_LAYERS, d, d), d ** -0.5),
        "b_rel_bias": nrm(ks[7], (N_B_LAYERS, B_HEADS, 2 * MAX_REL_DIST + 1), 0.2),
        "b_w_o": nrm(ks[8], (N_B_LAYERS, d, d), d ** -0.5 * DEEPNORM_BETA),
        "ln_g": 1.0 + nrm(ks[9], (DEPTH, 2, d), 0.02),
        "ln_b": nrm(ks[10], (DEPTH, 2, d), 0.02),
        "ffn_w_in": nrm(ks[11], (DEPTH, d, 2 * D_FF), d ** -0.5),
        "ffn_w_out": nrm(ks[12], (DEPTH, D_FF, d), D_FF ** -0.5 * DEEPNORM_BETA),
    }

def first_block(x, a_w_qkv, a_lambda, a_subln_g, a_w_o, kv_w, b_w_q, b_rel_bias, b_w_o,
              ln_g, ln_b, ffn_w_in, ffn_w_out):
    k_band = v_band = band_valid = None
    for l in range(DEPTH):
        if l < N_A_LAYERS:
            mix = diff_attention(x, a_w_qkv[l], a_lambda[l], a_subln_g[l], a_w_o[l],
                                 lambda_init_fn(l))
        else:
            if l == N_A_LAYERS:
                k_band, v_band, band_valid = shared_kv_band(x, kv_w)
            j = l - N_A_LAYERS
            mix = chunk_attention(x, k_band, v_band, band_valid, b_w_q[j], b_rel_bias[j], b_w_o[j])
        x = layer_norm(DEEPNORM_ALPHA * x + mix, ln_g[l, 0], ln_b[l, 0])
        x = layer_norm(DEEPNORM_ALPHA * x + swiglu(x, ffn_w_in[l], ffn_w_out[l]), ln_g[l, 1], ln_b[l, 1])
    return x


DEPTH_2 = 1

D_MIX = D_MODEL
D_A = D_MIX // 2
D_B = D_MIX - D_A
A_HEADS_2 = 4
A_BLOCK = 128
A_HEAD_DIM_2 = D_A // A_HEADS_2
B_HEADS_2 = 4
B_DK = D_B // 2
B_DV = D_B
B_HEAD_K = B_DK // B_HEADS_2
B_HEAD_V = B_DV // B_HEADS_2
B_GATE_RANK = 16
B_GATE_TAU = 16.0
D_FF_2 = 4 * D_MODEL
D_IN = 2 * D_A + 2 * B_DK + 2 * B_DV + B_GATE_RANK
EPS = 1e-6


def rmsnorm(x, g):
    xf = x.astype(jnp.float32)
    xf = xf * lax.rsqrt(jnp.mean(xf * xf, axis=-1, keepdims=True) + EPS)
    return (xf * g.astype(jnp.float32)).astype(x.dtype)

def layernorm(x, g, b):
    xf = x.astype(jnp.float32)
    mu = jnp.mean(xf, axis=-1, keepdims=True)
    xc = xf - mu
    xf = xc * lax.rsqrt(jnp.mean(xc * xc, axis=-1, keepdims=True) + EPS)
    return (xf * g.astype(jnp.float32) + b.astype(jnp.float32)).astype(x.dtype)

def gmlp_mixer(zu, zv, ln_g, ln_b, ws, bs, out_g):
    bsz, s, _ = zu.shape
    u = jax.nn.gelu(zu)
    v = layernorm(jax.nn.gelu(zv), ln_g, ln_b)
    n_blk = s // A_BLOCK
    v = v.reshape(bsz, n_blk, A_BLOCK, A_HEADS_2, A_HEAD_DIM_2)
    pos = jnp.arange(A_BLOCK) // CHUNK
    mask = pos[:, None] >= pos[None, :]
    w = jnp.where(mask[None], ws, jnp.zeros_like(ws))
    mixed = jnp.einsum('hij,bnjhc->bnihc', w, v) + jnp.transpose(bs)[None, None, :, :, None]
    out = u * mixed.reshape(bsz, s, D_A)
    return rmsnorm(out, out_g)

def gla_mixer(zq, zk, zv, zg, zlr, gate_w, gate_b, out_g):
    dt = zq.dtype
    bsz, s, _ = zq.shape
    n_c = s // CHUNK
    f32 = jnp.float32
    q = zq.astype(f32) * (B_HEAD_K ** -0.5)
    k = zk.astype(f32)
    v = zv.astype(f32)
    log_a = jax.nn.log_sigmoid(zlr.astype(f32) @ gate_w.astype(f32) + gate_b.astype(f32)) / B_GATE_TAU

    def to_chunks(t, d):
        return jnp.transpose(t.reshape(bsz, n_c, CHUNK, B_HEADS_2, d), (0, 3, 1, 2, 4))

    q, k, log_a = to_chunks(q, B_HEAD_K), to_chunks(k, B_HEAD_K), to_chunks(log_a, B_HEAD_K)
    v = to_chunks(v, B_HEAD_V)
    cum = jnp.cumsum(log_a, axis=-2)
    last = cum[..., -1:, :]
    qe = q * jnp.exp(cum)
    ke = k * jnp.exp(-cum)
    kd = k * jnp.exp(last - cum)

    tril = jnp.tril(jnp.ones((CHUNK, CHUNK), dtype=bool))
    scores = jnp.einsum('bhnid,bhnjd->bhnij', qe, ke)
    scores = jnp.where(tril, scores, 0.0)
    o_intra = jnp.einsum('bhnij,bhnjv->bhniv', scores, v)

    upd = jnp.einsum('bhnjd,bhnjv->bhndv', kd, v)
    dec = jnp.exp(last[..., 0, :])

    def step(state, inp):
        d_c, u_c = inp
        return d_c[..., None] * state + u_c, state

    s0 = jnp.zeros((bsz, B_HEADS_2, B_HEAD_K, B_HEAD_V), f32)
    _, s_prev = lax.scan(step, s0, (jnp.moveaxis(dec, 2, 0), jnp.moveaxis(upd, 2, 0)))
    s_prev = jnp.moveaxis(s_prev, 0, 2)
    o_inter = jnp.einsum('bhnid,bhndv->bhniv', qe, s_prev)

    o = jnp.transpose(o_intra + o_inter, (0, 2, 3, 1, 4))
    o = o.reshape(bsz, s, B_HEADS_2, B_HEAD_V)
    o = rmsnorm(o, out_g.reshape(B_HEADS_2, B_HEAD_V)).reshape(bsz, s, B_DV)
    return (o * jax.nn.silu(zg.astype(f32))).astype(dt)

def second_inputs(seed: int = 0) -> dict:
    key = jax.random.key(seed)
    ks = jax.random.split(key, 20)
    n = jax.random.normal

    def gain(k, d):
        return 1.0 + 0.05 * n(k, (DEPTH_2, d), jnp.float32)

    return {
        "x": n(ks[0], (BATCH, SEQ, D_MODEL), jnp.float32),
        "pre_mix_g": gain(ks[1], D_MODEL),
        "w_in": n(ks[2], (DEPTH_2, D_MODEL, D_IN), jnp.float32) * D_MODEL ** -0.5,
        "gmlp_ln_g": gain(ks[3], D_A),
        "gmlp_ln_b": 0.02 * n(ks[4], (DEPTH_2, D_A), jnp.float32),
        "gmlp_ws": n(ks[5], (DEPTH_2, A_HEADS_2, A_BLOCK, A_BLOCK), jnp.float32) * A_BLOCK ** -0.5,
        "gmlp_bs": 1.0 + 0.1 * n(ks[6], (DEPTH_2, A_HEADS_2, A_BLOCK), jnp.float32),
        "gmlp_out_g": gain(ks[7], D_A),
        "gla_gate_w": n(ks[8], (DEPTH_2, B_GATE_RANK, B_DK), jnp.float32) * B_GATE_RANK ** -0.5,
        "gla_gate_b": 0.5 * n(ks[9], (DEPTH_2, B_DK), jnp.float32),
        "gla_out_g": gain(ks[10], B_DV),
        "w_out": n(ks[11], (DEPTH_2, D_MIX, D_MODEL), jnp.float32) * D_MIX ** -0.5,
        "post_mix_g": gain(ks[12], D_MODEL),
        "pre_ff_g": gain(ks[13], D_MODEL),
        "w_ff1": n(ks[14], (DEPTH_2, D_MODEL, D_FF_2), jnp.float32) * D_MODEL ** -0.5,
        "w_ff2": n(ks[15], (DEPTH_2, D_FF_2, D_MODEL), jnp.float32) * D_FF_2 ** -0.5,
        "post_ff_g": gain(ks[16], D_MODEL),
    }

def second_block(x, pre_mix_g, w_in, gmlp_ln_g, gmlp_ln_b, gmlp_ws, gmlp_bs, gmlp_out_g,
              gla_gate_w, gla_gate_b, gla_out_g, w_out, post_mix_g, pre_ff_g,
              w_ff1, w_ff2, post_ff_g):
    cuts = [D_A, 2 * D_A, 2 * D_A + B_DK, 2 * D_A + 2 * B_DK,
            2 * D_A + 2 * B_DK + B_DV, 2 * D_A + 2 * B_DK + 2 * B_DV]
    h = x
    for l in range(DEPTH_2):
        y = rmsnorm(h, pre_mix_g[l])
        z = y @ w_in[l]
        zu, zv, zq, zk, zvb, zg, zlr = jnp.split(z, cuts, axis=-1)
        a = gmlp_mixer(zu, zv, gmlp_ln_g[l], gmlp_ln_b[l], gmlp_ws[l], gmlp_bs[l], gmlp_out_g[l])
        b = gla_mixer(zq, zk, zvb, zg, zlr, gla_gate_w[l], gla_gate_b[l], gla_out_g[l])
        m = jnp.concatenate([a, b], axis=-1) @ w_out[l]
        h = h + rmsnorm(m, post_mix_g[l])
        f = rmsnorm(h, pre_ff_g[l]) @ w_ff1[l]
        f = jnp.square(jax.nn.relu(f)) @ w_ff2[l]
        h = h + rmsnorm(f, post_ff_g[l])
    return h


def setup_inputs(seed=0):
    out = dict(first_inputs(seed))
    for name, value in second_inputs(seed + 1).items():
        if name != "x":
            out[name + "_2"] = value
    return out


def reference(
    x, a_w_qkv, a_lambda, a_subln_g, a_w_o, kv_w, b_w_q, b_rel_bias, b_w_o, ln_g, ln_b,
    ffn_w_in, ffn_w_out, pre_mix_g_2, w_in_2, gmlp_ln_g_2, gmlp_ln_b_2, gmlp_ws_2, gmlp_bs_2,
    gmlp_out_g_2, gla_gate_w_2, gla_gate_b_2, gla_out_g_2, w_out_2, post_mix_g_2, pre_ff_g_2,
    w_ff1_2, w_ff2_2, post_ff_g_2,
):
    x = first_block(
        x, a_w_qkv, a_lambda, a_subln_g, a_w_o, kv_w, b_w_q, b_rel_bias, b_w_o, ln_g, ln_b,
        ffn_w_in, ffn_w_out,
    )
    return second_block(
        x, pre_mix_g_2, w_in_2, gmlp_ln_g_2, gmlp_ln_b_2, gmlp_ws_2, gmlp_bs_2, gmlp_out_g_2,
        gla_gate_w_2, gla_gate_b_2, gla_out_g_2, w_out_2, post_mix_g_2, pre_ff_g_2, w_ff1_2,
        w_ff2_2, post_ff_g_2,
    )


_drawn_inputs = setup_inputs


def setup_inputs(seed=0):
    import zlib

    import numpy as np

    out = dict(_drawn_inputs(seed))
    spreads = {}
    factors = {'a_subln_g': 6.804,
     'b_rel_bias': 5.287,
     'gmlp_ln_g_2': 10.06,
     'gmlp_ln_b_2': 24.146,
     'gla_out_g_2': 2.927,
     'gmlp_bs_2': 3.905,
     'gmlp_out_g_2': 3.164}
    for name, (base, spread) in spreads.items():
        noise = np.random.default_rng([zlib.crc32(name.encode()), seed]).standard_normal(out[name].shape)
        drawn = base * np.exp(spread * noise) if base else spread * noise
        out[name] = __import__('jax').numpy.asarray(drawn.astype(out[name].dtype))
    for name, factor in factors.items():
        out[name] = (out[name] * factor).astype(out[name].dtype)
    return out
```

```python
import math
from contextlib import ExitStack

import numpy as np

import concourse.bass as bass
from concourse import mybir

F32 = mybir.dt.float32
F32R = mybir.dt.float32r
ALU = mybir.AluOpType
ACT = mybir.ActivationFunctionType
AX = mybir.AxisListType.X

D = 1024
S = 512
FF = 2816
FF2 = 4096
NEG = float(np.finfo(np.float32).min)
ALPHA = 4 ** 0.25
LAMBDA_INIT = 0.8 - 0.6 * math.exp(0.0)
ELEN = 640


class Count:

    def __init__(self, sem):
        self.sem, self.value = sem, 0

    def add(self, n):
        self.value += n
        return (self, self.value)


def flat(waits):
    for w in waits:
        if w is None:
            continue
        if isinstance(w, list):
            yield from flat(w)
        else:
            yield w


class Queue:

    def __init__(self, count):
        self.count, self.items, self.waited = count, [], {}

    def wait(self, *tokens):
        for count, value in flat(tokens):
            if self.waited.get(count, 0) < value:
                self.waited[count] = value
                self.items.append(lambda e, c=count, v=value: e.wait_ge(c.sem, v))

    def op(self, issue, *tokens):
        self.wait(*tokens)
        self.items.append(lambda e: issue(e).then_inc(self.count.sem, 1))
        return self.count.add(1)

    def quiet(self, issue, *tokens):
        self.wait(*tokens)
        self.items.append(issue)

    def dma(self, count, out, in_, *tokens, slow=False):
        self.wait(*tokens)
        self.items.append(lambda e: e.dma_start(out, in_, allow_slow_non_contiguous=slow).then_inc(count.sem, 16))
        return count.add(16)

    def play(self, engine):
        for item in self.items:
            item(engine)


def f32(ap):
    return ap.bitcast(F32)


def weave(main, fill):
    done = 0
    for i, item in enumerate(main):
        upto = len(fill) * (i + 1) // (len(main) + 1)
        while done < upto:
            fill[done]()
            done += 1
        item()
    for item in fill[done:]:
        item()


def build(nc, ap, out, upto=99):
    with ExitStack() as ctx:
        def sb(name, shape, dt=F32):
            return ctx.enter_context(nc.sbuf_tensor(name, shape, dt))

        def count(name):
            return Count(ctx.enter_context(nc.semaphore(name)))

        PE, AC, DV, PL, SP = (Queue(count("s_" + n)) for n in ("pe", "act", "dve", "pool", "sp"))

        ps = [ctx.enter_context(nc.psum_tensor(f"ps{i}", [128, 512], F32)) for i in range(8)]
        RING = 4
        raw = sb("raw", [128, RING, 1024])
        whi = sb("whi", [128, RING, 1024], F32R)
        wlo = sb("wlo", [128, RING, 1024], F32R)
        x = sb("x", [128, 4, D])
        xh = sb("xh", [128, 8, S], F32R)
        xl = sb("xl", [128, 8, S], F32R)
        hh = sb("hh", [128, 8, S], F32R)
        hl = sb("hl", [128, 8, S], F32R)
        arena = sb("arena", [128, 19200])
        ident = sb("ident", [128, 128])
        ones = sb("ones", [128, 128])
        stat = sb("stat", [128, 512])
        small = sb("small", [128, 128])

        def ar(start, n):
            return arena[:, start:start + n]

        rest = [None] * 8
        turn = [0]
        held = set()

        def bank(hold=False):
            while turn[0] % 8 in held:
                turn[0] += 1
            b = turn[0] % 8
            turn[0] += 1
            if hold:
                held.add(b)
            return b

        def let_go(b, token):
            held.discard(b)
            rest[b] = token

        eps5, eps6 = small[:, 0:1], small[:, 1:2]
        nlam, g8 = small[:, 2:3], small[:, 3:4]
        mask0, mask1 = small[:, 4:5], small[:, 5:6]
        gocol, blcol = small[:, 6:10], small[:, 10:14]
        dec = small[:, 16:32]
        bst = small[:, 32:80]
        mv = small[:, 80:88]
        rs = small[:, 88:96]
        lsum = small[:, 96:104]

        c_in = [count(f"s_in{i}") for i in range(12)]
        c_x = [count(f"s_x{i}") for i in range(4)]
        for t in range(4):
            SP.dma(c_x[t], x[:, t, :], ap["x"][0, t * 128:(t + 1) * 128, :])
            xw0 = None
        t_ident = SP.dma(c_in[0], ident[:], ap["c_ident"])
        x_in = [(c_x[t], 16) for t in range(4)]

        def last_pool():
            return (PL.count, PL.count.value)

        t_ones = PL.op(lambda e: e.memset(ones[:], 1.0))
        t_eps5 = PL.op(lambda e: e.memset(eps5, 1e-5), last_pool())
        t_eps6 = PL.op(lambda e: e.memset(eps6, 1e-6), last_pool())

        plan = []

        def plan_cols(w, c0, n=8, k0=0):
            plan.append((w[k0 * 128:(k0 + n) * 128, c0:c0 + 128], n, 128))

        def plan_rows(w, k0, c0):
            plan.append((w[k0 * 128:(k0 + 2) * 128, c0:c0 + 512], 2, 512))

        def plan_out(w, k0, nk):
            for nh in range(2):
                for k in range(k0, k0 + nk, 2):
                    plan_rows(w, k, nh * 512)

        qkv, kvw, bq = ap["a_w_qkv"][0], ap["kv_w"], ap["b_w_q"][0]
        win2 = ap["w_in_2"][0]
        groups = [(0, 8), (8, 8), (16, 6)]
        for nh in range(2):
            for k in range(0, 8, 2):
                plan_rows(qkv, k, 2048 + nh * 512)
        for h in range(8):
            plan_cols(qkv, h * 128)
            plan_cols(qkv, 1024 + h * 128)
        plan_out(ap["a_w_o"][0], 0, 8)

        def plan_ffn(layer):
            for f0, nf in groups:
                for f in range(f0, f0 + nf):
                    plan_cols(ap["ffn_w_in"][layer], f * 128)
                    plan_cols(ap["ffn_w_in"][layer], FF + f * 128)
                plan_out(ap["ffn_w_out"][layer], f0, nf)

        plan_ffn(0)
        for nh in range(2):
            for k in range(0, 8, 2):
                plan_rows(kvw, k, 1024 + nh * 512)
        for p in range(8):
            plan_cols(bq, p * 128)
            plan_cols(kvw, p * 128)
        plan_out(ap["b_w_o"][0], 0, 8)
        plan_ffn(1)
        zlr_at = len(plan)
        plan_cols(win2, 2448)
        for c in (1280, 1408, 1024, 1152):
            plan_cols(win2, c)
        for c in (1536, 512):
            for k in range(0, 8, 2):
                plan_rows(win2, k, c)
        for c in range(4):
            plan_cols(win2, 2048 + c * 128)
        for c in range(4):
            plan_cols(win2, c * 128)
        plan_out(ap["w_out_2"][0], 0, 8)
        for g in range(4):
            for f in range(8):
                plan_cols(ap["w_ff1_2"][0], (g * 8 + f) * 128)
            plan_out(ap["w_ff2_2"][0], g * 8, 8)

        class Weights:
            def __init__(self):
                self.c = [count(f"s_w{i}") for i in range(RING)]
                self.loaded, self.split_n, self.taken = 0, 0, 0
                self.dma_t, self.hi_t, self.lo_t, self.done_t = {}, {}, {}, {}
                while self.loaded < RING:
                    self.load()

            def load(self):
                j = self.loaded
                if j >= len(plan):
                    return
                src, n, cols = plan[j]
                s = j % RING
                dst = raw[:, s, :].rearrange("p (k c) -> p k c", k=n)
                free = [self.hi_t.get(j - RING), self.lo_t.get(j - RING)]
                if j == zlr_at:
                    view = win2.rearrange("(k p) c -> p k c", p=128)
                    SP.dma(self.c[s], dst[:, :, 0:16], view[:, :, 2560:2576], free)
                    t = SP.dma(self.c[s], dst[:, :, 16:128], view[:, :, 2448:2560])
                else:
                    t = SP.dma(self.c[s], dst, src.rearrange("(k p) c -> p k c", p=128), free)
                self.dma_t[j] = t
                self.loaded += 1

            def pump(self):
                while self.split_n < min(len(plan), self.taken + RING - 1):
                    j = self.split_n
                    if j >= RING and j - RING not in self.done_t:
                        return
                    s = j % RING
                    free = self.done_t.get(j - RING)
                    self.hi_t[j] = AC.op(lambda e, s=s: e.activation(whi[:, s, :], raw[:, s, :], ACT.Copy),
                                         self.dma_t[j], free)
                    self.lo_t[j] = DV.op(lambda e, s=s: e.tensor_tensor(wlo[:, s, :], raw[:, s, :],
                                                                        f32(whi[:, s, :]), ALU.subtract),
                                         self.dma_t[j], self.hi_t[j], free)
                    self.split_n += 1
                    self.load()

            def take(self):
                j = self.taken
                self.taken += 1
                self.pump()
                assert j < self.split_n
                _, n, cols = plan[j]
                s = j % RING
                h = whi[:, s, :].rearrange("p (k c) -> p k c", k=n)
                low = wlo[:, s, :].rearrange("p (k c) -> p k c", k=n)
                return j, h, low, [self.hi_t[j], self.lo_t[j]]

            def done(self, j, token):
                self.done_t[j] = token
                self.pump()

        W = Weights()
        W.pump()

        def mm3(e, o, ah, al, bh, bl, start, stop):
            e.matmul(o, ah, bh, start=start, stop=False)
            e.matmul(o, ah, bl, start=False, stop=False)
            return e.matmul(o, al, bh, start=False, stop=stop)

        x_ready = []
        h_ready = [None] * 8

        def project(post):
            st = {}

            def piece(i):
                if i == 0:
                    st["w"] = W.take()
                    st["b"] = bank(hold=True)
                j, wh, wl, ready = st["w"]
                b = st["b"]

                def issue(e):
                    for k in (2 * i, 2 * i + 1):
                        m = mm3(e, ps[b][:], wh[:, k, :], wl[:, k, :], xh[:, k, :], xl[:, k, :], k == 0, k == 7)
                    return m

                if i < 3:
                    PE.quiet(issue, *([ready, rest[b], x_ready] if i == 0 else []))
                else:
                    t = PE.op(issue)
                    W.done(j, t)
                    held.discard(b)
                    post(b, t)

            return [lambda i=i: piece(i) for i in range(4)]

        def tokens_out(post, ah, al, ready_of, nk, k_first=0):
            later = []
            for nh in range(2):
                banks = [bank() for _ in range(4)]
                n_last = min(3, nk // 2) if nh == 1 else 1
                for k0 in range(0, nk - 2 * n_last, 2):
                    j, wh, wl, ready = W.take()
                    for t in range(4):
                        def issue(e, t=t, k0=k0, wh=wh, wl=wl, o=ps[banks[t]]):
                            for k in (0, 1):
                                a = slice(t * 128, t * 128 + 128)
                                m = mm3(e, o[:], ah[:, k0 + k, a], al[:, k0 + k, a],
                                        wh[:, k, :], wl[:, k, :], k0 + k == 0, False)
                            return m
                        need = [ready, rest[banks[t]] if k0 == 0 else None, ready_of(k0), ready_of(k0 + 1)]
                        if t == 3:
                            W.done(j, PE.op(issue, need))
                        else:
                            PE.quiet(issue, need)
                blocks = [W.take() for _ in range(n_last)]
                for t in range(4):
                    for n, (j, wh, wl, ready) in enumerate(blocks):
                        k0 = nk - 2 * n_last + 2 * n

                        def issue(e, t=t, k0=k0, wh=wh, wl=wl, o=ps[banks[t]]):
                            for k in (0, 1):
                                a = slice(t * 128, t * 128 + 128)
                                m = mm3(e, o[:], ah[:, k0 + k, a], al[:, k0 + k, a],
                                        wh[:, k, :], wl[:, k, :], k0 + k == 0, k0 + k == nk - 1)
                            return m
                        need = [ready, rest[banks[t]] if k0 == 0 else None, ready_of(k0), ready_of(k0 + 1)]
                        if t == 3 or n == n_last - 1:
                            token = PE.op(issue, need)
                            if t == 3:
                                W.done(j, token)
                        else:
                            PE.quiet(issue, need)
                    for f in later:
                        f()
                    later = []
                    more = post(nh, t, banks[t], token)
                    if more:
                        later.append(more)
            for f in later:
                f()

        def to_features(t, src, ready):
            tokens = []
            for half in range(2):
                b = bank()

                def issue(e, half=half, b=b):
                    for k in range(4):
                        m = e.transpose(ps[b][:, k * 128:(k + 1) * 128],
                                        src[:, (half * 4 + k) * 128:(half * 4 + k + 1) * 128], ident[:])
                    return m
                tr = PE.op(issue, ready, rest[b], t_ident)
                dst = (slice(None), slice(half * 4, half * 4 + 4), slice(t * 128, t * 128 + 128))
                view = ps[b][:].rearrange("p (k c) -> p k c", k=4)
                hi = AC.op(lambda e, dst=dst, view=view: e.activation(xh[dst], view, ACT.Copy), tr)
                lo = DV.op(lambda e, dst=dst, view=view: e.tensor_tensor(xl[dst], view, f32(xh[dst]), ALU.subtract), hi)
                rest[b] = lo
                tokens += [hi, lo]
            return tokens

        def moments(t, part, src, ready):
            return DV.op(lambda e: e.bn_stats(bst[:, t * 12 + part * 6:t * 12 + part * 6 + 6], src), ready)

        def inv_std(t, parts, eps, t_eps, plain, ready):
            m, r = mv[:, 2 * t:2 * t + 2], rs[:, t:t + 1]
            a = DV.op(lambda e: e.bn_aggr(m, bst[:, t * 12:t * 12 + 6 * parts]), ready)
            if not plain:
                a = DV.op(lambda e: e.scalar_tensor_tensor(m[:, 1:2], m[:, 0:1], m[:, 0:1], m[:, 1:2],
                                                           ALU.mult, ALU.add), a)
            s = AC.op(lambda e: e.activation(lsum[:, t:t + 1], m[:, 1:2], ACT.Sqrt, bias=eps), a, t_eps)
            return DV.op(lambda e: e.reciprocal(r, lsum[:, t:t + 1]), s)

        gvec = [ar(i * 1024, 1024) for i in range(3)]
        c_g = [count(f"s_g{i}") for i in range(3)]

        def load_g(i, v, *free):
            src = bass.AP(tensor=v.tensor, offset=v.offset, ap=[[0, 128], [1, 1024]])
            return SP.dma(c_g[i], gvec[i], src, *free)

        last_g = [None, None, None]

        def layer_norm(t, ready, tg, tb):
            r = inv_std(t, 2, eps5, t_eps5, True, ready)
            a = DV.op(lambda e: e.scalar_tensor_tensor(x[:, t, :], x[:, t, :], mv[:, 2 * t:2 * t + 1], gvec[0],
                                                       ALU.subtract, ALU.mult), r, tg)
            a = DV.op(lambda e: e.scalar_tensor_tensor(x[:, t, :], x[:, t, :], rs[:, t:t + 1], gvec[1],
                                                       ALU.mult, ALU.add), a, tb)
            return a

        def residual_norm(i, last_group=True, first_group=True, after=None, vecs=None):
            first = {}
            ready = []

            def post(nh, t, b, token):
                cols = slice(nh * 512, nh * 512 + 512)
                scale = ALPHA if first_group else 1.0
                a = DV.op(lambda e: e.scalar_tensor_tensor(x[:, t, cols], x[:, t, cols], scale, ps[b][:],
                                                           ALU.mult, ALU.add), token)
                rest[b] = a
                if not last_group:
                    return None
                m = moments(t, nh, x[:, t, cols], a)
                if nh == 0:
                    return None
                return after(t, m)
            return post

        def norm_then_features(ln, row):
            l, r = divmod(row, 2)
            tg = load_g(0, ap["ln_g"][l, r], last_g[0])
            tb = load_g(1, ap["ln_b"][l, r], last_g[1])
            fresh = []

            def after(t, m):
                a = layer_norm(t, m, tg, tb)
                last_g[0] = last_g[1] = a

                def pe():
                    fresh.extend(to_features(t, x[:, t, :], a))
                return pe
            return after, fresh

        for t in range(4):
            x_ready += to_features(t, x[:, t, :], x_in[t])

        BASE = 3072

        def values_out(base, V):
            tokens = []

            def post(nh, t, b, token):
                a = AC.op(lambda e: e.activation(V[:, t, nh * 512:nh * 512 + 512], ps[b][:], ACT.Copy), token)
                rest[b] = a
                tokens.append(a)
                return None
            tokens_out(post, xh, xl, lambda k: x_ready, 8)
            return tokens

        def attention_a():
            cosb, sinb = ar(BASE, 512), ar(BASE + 512, 512)
            qk = [[ar(BASE + 1024 + (n * 3 + i) * 512, 512) for i in range(3)] for n in range(2)]
            V = ar(BASE + 4096, 4096).rearrange("p (t c) -> p t c", t=4)
            ebuf = [[ar(BASE + 8192 + (n * 2 + m) * 512, 512) for m in range(2)] for n in range(2)]
            aT = ar(BASE + 10240, 2048).rearrange("p (j q) -> p j q", j=4)
            tmp, sq, of = (ar(BASE + 12288 + i * 512, 512) for i in range(3))
            lam4 = ar(BASE + 12288, 256)
            t_cos = SP.dma(c_in[1], cosb, ap["c_cos"])
            t_sin = SP.dma(c_in[1], sinb, ap["c_sin"])
            t_mask = SP.dma(c_in[2], small[:, 4:6], ap["c_mask"])
            t_sub = SP.dma(c_in[3], g8, ap["a_subln_g"][0].rearrange("(p a) -> p a", a=1), slow=True)
            lp = ap["a_lambda"][0]
            t_lam = SP.dma(c_in[4], lam4, bass.AP(tensor=lp.tensor, offset=lp.offset, ap=[[0, 128], [1, 256]]))
            t_g8 = DV.op(lambda e: e.tensor_scalar(g8, g8, 1.0 - LAMBDA_INIT, None, ALU.mult), t_sub)
            l1 = DV.op(lambda e: e.tensor_tensor_reduce(sq[:, 0:64], lam4[:, 0:64], lam4[:, 64:128], 1.0, 0.0,
                                                        ALU.mult, ALU.add, lsum[:, 0:1]), t_lam)
            l2 = DV.op(lambda e: e.tensor_tensor_reduce(sq[:, 64:128], lam4[:, 128:192], lam4[:, 192:256], 1.0, 0.0,
                                                        ALU.mult, ALU.add, lsum[:, 1:2]), t_lam)
            le = AC.op(lambda e: e.activation(lsum[:, 2:4], lsum[:, 0:2], ACT.Exp), l1, l2)
            l3 = DV.op(lambda e: e.tensor_tensor(nlam, lsum[:, 3:4], lsum[:, 2:3], ALU.subtract), le)
            t_nlam = DV.op(lambda e: e.tensor_scalar(nlam, nlam, -LAMBDA_INIT, None, ALU.add), l3)

            v_ready = values_out(0, V)
            qk_ready = {}
            qk_free = {}

            def rope(h, which):
                def post(b, t):
                    q0, q1, k = qk[h % 2]
                    dst = k if which else q0
                    a = DV.op(lambda e: e.tensor_tensor(dst, ps[b][:], cosb, ALU.mult), t, t_cos, t_sin,
                              qk_free.get(h - 2))
                    DV.wait(t_nlam)
                    u0 = DV.op(lambda e: e.tensor_tensor(tmp[0:64, :], ps[b][64:128, :], sinb[64:128, :], ALU.mult))
                    u1 = DV.op(lambda e: e.tensor_tensor(tmp[64:128, :], ps[b][0:64, :], sinb[0:64, :], ALU.mult))
                    rest[b] = u1
                    s = DV.op(lambda e: e.tensor_tensor(dst, dst, tmp, ALU.add), a, u0, u1)
                    if not which:
                        q1t = DV.op(lambda e: e.tensor_scalar(q1, q0, mask1, None, ALU.mult), s, t_mask)
                        s = DV.op(lambda e: e.tensor_scalar(q0, q0, mask0, None, ALU.mult), q1t)
                    qk_ready.setdefault(h, []).append(s)
                return post

            a_ready, tr_done, at_ready = {}, {}, {}

            def scores(h, i):
                q0, q1, k = qk[h % 2]
                n = (i + 1) * 128
                c = (h * 4 + i) * 8
                mx, nb = stat[:, c:c + 2], stat[:, c + 2:c + 4]
                ls, r = stat[:, c + 4:c + 6], stat[:, c + 6:c + 8]
                buf = (h * 4 + i) % 2
                maxes, banks = [], []
                for m, q in enumerate((q0, q1)):
                    b = bank()
                    banks.append(b)
                    t = PE.op(lambda e, q=q, b=b: e.matmul(ps[b][:, 0:n], q[:, i * 128:i * 128 + 128], k[:, 0:n],
                                                           start=True, stop=True), qk_ready[h], rest[b])
                    qk_free[h] = t
                    t = DV.op(lambda e, b=b: e.memset(ps[b][0:64, n - 64:n], NEG), t)
                    maxes.append(DV.op(lambda e, b=b, m=m: e.reduce_max(mx[:, m:m + 1], ps[b][:, 0:n], AX), t))
                t = DV.op(lambda e: e.tensor_scalar(nb, mx, -0.125, None, ALU.mult), maxes)
                exps = []
                for m in range(2):
                    b = banks[m]
                    exps.append(AC.op(lambda e, m=m, b=b: e.activation(
                        ebuf[buf][m][:, 0:n], ps[b][:, 0:n], ACT.Exp, bias=nb[:, m:m + 1], scale=0.125,
                        accum_out=ls[:, m:m + 1]), t, tr_done.get((h * 4 + i) - 2)))
                    rest[b] = exps[-1]
                t = DV.op(lambda e: e.reciprocal(r, ls), exps)
                r1 = DV.op(lambda e: e.tensor_tensor(r[:, 1:2], r[:, 1:2], nlam, ALU.mult), t, t_nlam)
                e0, e1 = ebuf[buf][0][:, 0:n], ebuf[buf][1][:, 0:n]
                t = DV.op(lambda e: e.tensor_scalar(e0, e0, r[:, 0:1], None, ALU.mult), t)
                a_ready[h, i] = DV.op(lambda e: e.scalar_tensor_tensor(e0, e1, r[:, 1:2], e0, ALU.mult, ALU.add), t, r1)

            def turn_over(h, i):
                buf = (h * 4 + i) % 2
                e0 = ebuf[buf][0]
                b = bank()

                def issue(e):
                    for j in range(i + 1):
                        m = e.transpose(ps[b][:, j * 128:j * 128 + 128], e0[:, j * 128:j * 128 + 128], ident[:])
                    return m
                t = PE.op(issue, a_ready[h, i], rest[b])
                tr_done[h * 4 + i] = t
                n = (i + 1) * 128
                a = AC.op(lambda e: e.activation(aT[:, 0:i + 1, i * 128:i * 128 + 128],
                                                 ps[b][:, 0:n].rearrange("p (j q) -> p j q", j=i + 1), ACT.Copy), t)
                rest[b] = a
                at_ready[h, i] = a

            sq_free = [None]

            def weigh(h):
                b = bank(hold=True)

                def issue(e):
                    for j in range(4):
                        m = e.matmul(ps[b][:, j * 128:512], V[:, j, h * 128:h * 128 + 128], aT[:, j, j * 128:512],
                                     start=(j == 0), stop=(j == 3))
                    return m
                t = PE.op(issue, v_ready, rest[b], [at_ready[h, i] for i in range(4)])
                st[h] = (b, AC.op(lambda e: e.activation(sq, ps[b][:], ACT.Square), t, l1, l2, sq_free[0]))

            st = {}

            def norm(h):
                b, t = st[h]
                b2 = bank()
                m = PE.op(lambda e: e.matmul(ps[b2][:], ones[:], sq, start=True, stop=True), t, rest[b2], t_ones)
                a = AC.op(lambda e: e.activation(sq, ps[b2][:], ACT.Ln, bias=eps5, scale=1.0 / 128), m, t_eps5)
                rest[b2] = a
                a = AC.op(lambda e: e.activation(sq, sq, ACT.Exp, scale=-0.5), a)
                o = DV.op(lambda e: e.scalar_tensor_tensor(of, ps[b][:], g8, sq, ALU.mult, ALU.mult), a, t_g8,
                          h_ready[h - 1] if h else None)
                let_go(b, o)
                sq_free[0] = o
                hi = AC.op(lambda e: e.activation(hh[:, h, :], of, ACT.Copy), o)
                lo = DV.op(lambda e: e.tensor_tensor(hl[:, h, :], of, f32(hh[:, h, :]), ALU.subtract), hi)
                h_ready[h] = [hi, lo]

            def proj(h):
                return project(rope(h, 0)) + project(rope(h, 1))

            for f in proj(0):
                f()
            for h in range(9):
                items = []
                if h < 8:
                    items.append(lambda h=h: scores(h, 0))
                if h:
                    items.append(lambda h=h: turn_over(h - 1, 3))
                if h < 8:
                    items.append(lambda h=h: scores(h, 1))
                if h:
                    items.append(lambda h=h: weigh(h - 1))
                if h < 8:
                    items += [lambda h=h: turn_over(h, 0), lambda h=h: scores(h, 2), lambda h=h: turn_over(h, 1)]
                if h:
                    items.append(lambda h=h: norm(h - 1))
                if h < 8:
                    items += [lambda h=h: scores(h, 3), lambda h=h: turn_over(h, 2)]
                weave(items, proj(h + 1) if h < 7 else [])

        def ffn(layer, after_row, tail):
            sbuf_ = [ar(BASE + i * 512, 512) for i in range(2)]
            hbuf = [ar(BASE + 1024 + i * 512, 512) for i in range(2)]
            s_free, n = {}, [0]
            w_tail, fresh = None, None
            for gi, (f0, nf) in enumerate(groups):
                for f in range(nf):
                    st = {}

                    def post_gate(b, t, f=f):
                        i = n[0] % 2
                        st["s"] = AC.op(lambda e: e.activation(sbuf_[i], ps[b][:], ACT.Silu), t, s_free.get(n[0] - 2))
                        rest[b] = st["s"]

                    def post_up(b, t, f=f):
                        i = n[0] % 2
                        o = DV.op(lambda e: e.tensor_tensor(hbuf[i], ps[b][:], sbuf_[i], ALU.mult), t, st["s"],
                                  s_free.get(n[0] - 2))
                        rest[b] = o
                        hi = AC.op(lambda e: e.activation(hh[:, f, :], hbuf[i], ACT.Copy), o)
                        lo = DV.op(lambda e: e.tensor_tensor(hl[:, f, :], hbuf[i], f32(hh[:, f, :]), ALU.subtract), hi)
                        h_ready[f] = [hi, lo]
                        s_free[n[0]] = lo
                        n[0] += 1
                    if gi:
                        AC.wait(prev)
                        DV.wait(prev)
                    for piece in project(post_gate) + project(post_up):
                        piece()
                last = gi == len(groups) - 1
                if last:
                    after, fresh = tail(after_row)
                post = residual_norm(0, last, gi == 0, after if last else None)
                tokens_out(post, hh, hl, lambda k: h_ready[k], nf)
                prev = W.done_t[W.taken - 1]
            x_ready[:] = fresh

        esb = ar(BASE + 14336, 640)
        e2 = nc.dram_tensor("bias_rows", [16, ELEN], F32, kind="Internal").ap()
        toep = nc.dram_tensor("bias_skewed", [16, 128 * ELEN], F32, kind="Internal").ap()
        c_b = [count(f"s_b{i}") for i in range(5)]
        rel = ap["b_rel_bias"][0]
        t1 = SP.dma(c_b[0], esb[0:16, 256:640], rel[:, 1:385])
        t2 = SP.dma(c_b[0], esb[0:16, 0:2], rel[:, 0:2])
        t3 = PL.op(lambda e: e.tensor_copy(esb[0:16, 1:256], esb[0:16, 0:1].broadcast_to([16, 255])), t1, t2, last_pool())
        t4 = SP.dma(c_b[1], e2, esb[0:16, :], t3)
        src = bass.AP(tensor=e2.tensor, offset=0, ap=[[ELEN, 16], [0, 128], [1, ELEN]])
        dst = bass.AP(tensor=toep.tensor, offset=0, ap=[[128 * ELEN, 16], [ELEN, 128], [1, ELEN]])
        t_toep = SP.dma(c_b[2], dst, src, t4)

        attention_a()
        if upto == 1:
            o = [DV.op(lambda e, k=k: e.tensor_tensor(x[:, k // 2, (k % 2) * 512:(k % 2) * 512 + 512],
                                                     f32(hh[:, k, :]), f32(hl[:, k, :]), ALU.add), h_ready[k])
                 for k in range(8)]
            return finish(nc, locals(), o)

        after, fresh = norm_then_features(0, 0)
        tokens_out(residual_norm(0, True, True, after), hh, hl, lambda k: h_ready[k], 8)
        x_ready[:] = fresh
        if upto == 2:
            return finish(nc, locals(), x_ready)
        ffn(0, 1, lambda row: norm_then_features(0, row))
        if upto == 3:
            return finish(nc, locals(), x_ready)

        def attention_b():
            qk = [[ar(BASE + (n * 2 + i) * 512, 512) for i in range(2)] for n in range(2)]
            V = ar(BASE + 4096, 4096).rearrange("p (t c) -> p t c", t=4)
            ebuf = [ar(BASE + 8192 + n * 512, 512) for n in range(3)]
            PT = ar(BASE + 10240, 2048).rearrange("p (j q) -> p j q", j=4)
            bt = [ar(BASE + 2048 + n * 512, 512) for n in range(3)]
            v_ready = values_out(0, V)
            qk_ready, qk_free = {}, {}
            bt_ready, bt_free = {}, {}

            def load_bias(h):
                i = h % 3
                src = bass.AP(tensor=toep.tensor, offset=h * 128 * ELEN + 127, ap=[[ELEN - 1, 128], [1, 512]])
                t = SP.dma(c_b[3 + i] if i < 2 else c_b[0], bt[i], src, t_toep, bt_free.get(h - 3), v_ready)
                bt_ready[h] = PL.op(lambda e: e.memset(bt[i][0:64, 448:512], NEG), t, last_pool())

            def keep(p, which):
                def post(b, t):
                    if which:
                        s = AC.op(lambda e: e.activation(qk[p % 2][1], ps[b][:], ACT.Copy), t, qk_free.get(p - 2))
                    else:
                        s = AC.op(lambda e: e.activation(qk[p % 2][0], ps[b][:], ACT.Copy, scale=0.125), t,
                                  qk_free.get(p - 2))
                    rest[b] = s
                    qk_ready.setdefault(p, []).append(s)
                return post

            p_ready, tr_done, pt_ready = {}, {}, {}

            def scores(h, i):
                p, a = divmod(h, 2)
                q, k = qk[p % 2]
                n = (i + 1) * 128
                c = (h * 4 + i) * 4
                mx, nb, ls, r = (stat[:, c + z:c + z + 1] for z in range(4))
                s = h * 4 + i
                e_ = ebuf[s % 3][:, 0:n]
                rows = slice(64 * a, 64 * a + 64)
                b = bank()
                t = PE.op(lambda e: e.matmul(ps[b][:, 0:n], q[rows, i * 128:i * 128 + 128], k[rows, 0:n],
                                             start=True, stop=True), qk_ready[p], rest[b])
                qk_free[p] = t
                t = DV.op(lambda e: e.tensor_tensor_reduce(e_, ps[b][:, 0:n], bt[h % 3][:, 384 - 128 * i:512], 1.0, NEG,
                                                           ALU.add, ALU.max, mx), t, bt_ready[h], tr_done.get(s - 3))
                rest[b] = t
                bt_free[h] = t
                t = DV.op(lambda e: e.tensor_scalar(nb, mx, -1.0, None, ALU.mult), t)
                t = AC.op(lambda e: e.activation(e_, e_, ACT.Exp, bias=nb, accum_out=ls), t)
                t = DV.op(lambda e: e.reciprocal(r, ls), t)
                p_ready[s] = DV.op(lambda e: e.tensor_scalar(e_, e_, r, None, ALU.mult), t)

            def turn_over(h, i):
                s = h * 4 + i
                e_ = ebuf[s % 3]
                b = bank()

                def issue(e):
                    for j in range(i + 1):
                        m = e.transpose(ps[b][:, j * 128:j * 128 + 128], e_[:, j * 128:j * 128 + 128], ident[:])
                    return m
                t = PE.op(issue, p_ready[s], rest[b])
                tr_done[s] = t
                n = (i + 1) * 128
                pt_ready[h, i] = rest[b] = AC.op(lambda e: e.activation(
                    PT[:, 0:i + 1, i * 128:i * 128 + 128],
                    ps[b][:, 0:n].rearrange("p (j q) -> p j q", j=i + 1), ACT.Copy), t)

            ob = {}

            def weigh(h):
                p, a = divmod(h, 2)
                if not a:
                    ob[p] = bank(hold=True)
                b = ob[p]
                rows = slice(64 * a, 64 * a + 64)

                def issue(e):
                    for j in range(4):
                        m = e.matmul(ps[b][rows, j * 128:512], V[:, j, h * 64:h * 64 + 64], PT[:, j, j * 128:512],
                                     start=(j == 0), stop=(j == 3))
                    return m
                t = PE.op(issue, v_ready, rest[b], [pt_ready[h, i] for i in range(4)])
                if a:
                    hi = AC.op(lambda e: e.activation(hh[:, p, :], ps[b][:], ACT.Copy), t)
                    lo = DV.op(lambda e: e.tensor_tensor(hl[:, p, :], ps[b][:], f32(hh[:, p, :]), ALU.subtract), hi)
                    let_go(b, lo)
                    h_ready[p] = [hi, lo]

            def proj(p):
                return project(keep(p, 0)) + project(keep(p, 1))

            load_bias(0)
            load_bias(1)
            for f in proj(0):
                f()
            for p in range(9):
                items = []
                for a in range(2):
                    h = 2 * p + a
                    if h < 16:
                        items += [lambda h=h: scores(h, 0)]
                    if 0 < h <= 16:
                        items += [lambda h=h: turn_over(h - 1, 3)]
                    if h < 16:
                        items += [lambda h=h: scores(h, 1)]
                    if 0 < h <= 16:
                        items += [lambda h=h: weigh(h - 1)]
                    if h < 16:
                        if h + 2 < 16:
                            items.append(lambda h=h: load_bias(h + 2))
                        items += [lambda h=h: turn_over(h, 0), lambda h=h: scores(h, 2), lambda h=h: turn_over(h, 1),
                                  lambda h=h: scores(h, 3), lambda h=h: turn_over(h, 2)]
                weave(items, proj(p + 1) if p < 7 else [])

        attention_b()
        if upto == 4:
            o = [DV.op(lambda e, k=k: e.tensor_tensor(x[:, k // 2, (k % 2) * 512:(k % 2) * 512 + 512],
                                                     f32(hh[:, k, :]), f32(hl[:, k, :]), ALU.add), h_ready[k])
                 for k in range(8)]
            return finish(nc, locals(), o)
        after, fresh = norm_then_features(1, 2)
        tokens_out(residual_norm(0, True, True, after), hh, hl, lambda k: h_ready[k], 8)
        x_ready[:] = fresh

        yb = [ar(9216 + i * 1024, 1024) for i in range(2)]
        y_free = [None, None]

        def rms_features(t, tg, fresh, ready):
            m0 = moments(t, 0, x[:, t, 0:512], ready)
            m1 = moments(t, 1, x[:, t, 512:1024], ready)
            r = inv_std(t, 2, eps6, t_eps6, False, [m0, m1])
            y = yb[t % 2]
            a = DV.op(lambda e: e.scalar_tensor_tensor(y, x[:, t, :], rs[:, t:t + 1], gvec[2], ALU.mult, ALU.mult),
                      r, tg, y_free[t % 2])
            last_g[2] = a

            def pe():
                fresh.extend(to_features(t, y, a))
                y_free[t % 2] = (PE.count, PE.count.value)
            return pe

        def tail_two(row):
            l, r_ = divmod(row, 2)
            tg = load_g(0, ap["ln_g"][l, r_], last_g[0])
            tb = load_g(1, ap["ln_b"][l, r_], last_g[1])
            tp = load_g(2, ap["pre_mix_g_2"][0], last_g[2])
            fresh = []

            def after(t, m):
                a = layer_norm(t, m, tg, tb)
                last_g[0] = last_g[1] = a
                return rms_features(t, tp, fresh, a)
            return after, fresh
        ffn(1, 3, tail_two)
        if upto == 5:
            return finish(nc, locals(), x_ready)

        def mixer():
            v = ar(3072, 2048).rearrange("p (t c) -> p t c", t=4)
            vb = ar(5120, 2048).rearrange("p (t c) -> p t c", t=4)
            qe = [ar(7168 + p * 512, 512) for p in range(2)]
            ke = [ar(8192 + p * 512, 512) for p in range(2)]
            outa = ar(7168, 2048).rearrange("p (h q) -> p h q", h=4)
            la = ar(9216, 1024).rearrange("p (t c) -> p t c", t=4)
            cum = [ar(10240, 512), ar(10752, 512)]
            on = ar(9216, 2048).rearrange("p (h q) -> p h q", h=4)
            ex = [ar(11264, 512), ar(11776, 512)]
            sc = [ar(12288 + i * 512, 512).rearrange("p (t c) -> p t c", t=4) for i in range(2)]
            wT = ar(13312, 512).rearrange("p (h i) -> p h i", h=4)
            sq, rinv, of, ub = (ar(13824 + i * 512, 512) for i in range(4))
            wsb = ar(15872, 512).rearrange("p (h j) -> p h j", h=4)
            bsr = ar(16384, 512)
            gw, gb = ar(16896, 256), ar(17152, 512)
            zl = ar(17664, 512)
            lng, lnb = ar(18176, 512), ar(18688, 512)
            kd = [ar(p * 512, 512).rearrange("p (t c) -> p t c", t=4) for p in range(2)]
            St = ar(1024, 1792).rearrange("p (n c) -> p n c", n=14)
            tri = sb("tri", [128, 128])
            t_tri = SP.dma(c_in[5], tri[:], ap["c_tri"])
            wide = lambda u, n: bass.AP(tensor=u.tensor, offset=u.offset, ap=[[0, 128], [1, n]])
            SP.wait(x_ready)
            t_ws = SP.dma(c_in[6], wsb, ap["gmlp_ws_2"][0].rearrange("h i j -> i h j"))
            SP.dma(c_in[7], bsr[0:1, :], ap["gmlp_bs_2"].rearrange("a h i -> a (h i)"))
            SP.dma(c_in[7], gw[0:16, :], ap["gla_gate_w_2"][0])
            SP.dma(c_in[7], gb[0:1, 0:256], ap["gla_gate_b_2"])
            SP.dma(c_in[7], gb[0:1, 256:512], ap["gla_gate_b_2"])
            SP.dma(c_in[7], gocol, ap["gmlp_out_g_2"][0].rearrange("(h p) -> p h", p=128), slow=True)
            t_sm = SP.dma(c_in[7], blcol, ap["gla_out_g_2"][0].rearrange("(h p) -> p h", p=128), slow=True)
            SP.dma(c_in[8], lng, wide(ap["gmlp_ln_g_2"][0], 512))
            t_ln = SP.dma(c_in[8], lnb, wide(ap["gmlp_ln_b_2"][0], 512))

            tk = {}

            def post_zlr(b, t):
                tk["zl"] = rest[b] = AC.op(lambda e: e.activation(zl[0:16, :], ps[b][0:16, :], ACT.Copy), t)

            def keep(dst, name, scale=1.0):
                def post(b, t):
                    tk[name] = rest[b] = AC.op(lambda e: e.activation(dst, ps[b][:], ACT.Copy, scale=scale), t)
                return post

            def gate():
                for half in range(2):
                    b = bank()

                    def issue(e, half=half, b=b):
                        e.matmul(ps[b][:], ones[0:1, :], gb[0:1, :], start=True, stop=True,
                                 skip_group_check=True)
                        for i in range(2):
                            t = half * 2 + i
                            m = e.matmul(ps[b][:, i * 256:i * 256 + 256], zl[0:16, t * 128:t * 128 + 128], gw[0:16, :],
                                         start=False, stop=True, skip_group_check=True)
                        return m
                    t = PE.op(issue, tk["zl"], t_sm, rest[b], t_ones)
                    low = la[:, 2 * half:2 * half + 2, :].rearrange("p t c -> p (t c)")
                    ln = ex[half]
                    a = AC.op(lambda e, b=b, ln=ln: e.activation(ln, ps[b][:], ACT.Abs), t)
                    m = DV.op(lambda e, b=b, low=low: e.tensor_scalar(low, ps[b][:], 0.0, None, ALU.min), a)
                    rest[b] = m
                    a = AC.op(lambda e, ln=ln: e.activation(ln, ln, ACT.Exp, scale=-1.0), a)
                    a = AC.op(lambda e, ln=ln: e.activation(ln, ln, ACT.Ln, bias=1.0), a)
                    tk["la", half] = DV.op(lambda e, ln=ln, low=low: e.tensor_tensor(low, low, ln, ALU.subtract), m, a)

            def cumulate(p):
                b = bank()

                def issue(e):
                    for t in range(4):
                        m = e.matmul(ps[b][:, t * 128:t * 128 + 128], la[:, t, p * 128:p * 128 + 128], tri[:],
                                     start=True, stop=True)
                    return m
                t = PE.op(issue, tk["la", 0], tk["la", 1], t_tri, rest[b])
                tk["cum", p] = rest[b] = DV.op(lambda e: e.tensor_copy(cum[p], ps[b][:]), t)

            def decays(p):
                c3 = cum[p].rearrange("p (n i) -> p n i", n=8)
                x0, x1 = ex
                a = AC.op(lambda e: e.activation(x0, cum[p], ACT.Exp), tk["cum", p], tk["la", 0], tk["la", 1], tk.get("ex0"))
                d = DV.op(lambda e: e.tensor_copy(dec[:, p * 8:p * 8 + 8],
                                                  x0.rearrange("p (n i) -> p n i", n=8)[:, :, 63]), a)
                q = DV.op(lambda e: e.tensor_tensor(qe[p], qe[p], x0, ALU.mult), a, tk["q", p])
                tk["dec", p], tk["qe", p] = d, q
                l = DV.op(lambda e: e.tensor_tensor(x1.rearrange("p (n i) -> p n i", n=8),
                                                    c3[:, :, 63:64].broadcast_to([128, 8, 64]), c3, ALU.subtract),
                          tk["cum", p], tk["la", 0], tk["la", 1], tk.get("ex1"))
                l = AC.op(lambda e: e.activation(x1, x1, ACT.Exp), l)
                l = DV.op(lambda e: e.tensor_tensor(x1, x1, ke[p], ALU.mult), l, tk["k", p])
                tk["kdT", p] = l
                a = AC.op(lambda e: e.activation(x0, cum[p], ACT.Exp, scale=-1.0), d, q)
                tk["ke", p] = tk["ex0"] = DV.op(lambda e: e.tensor_tensor(ke[p], ke[p], x0, ALU.mult), a, l)
                b = bank()

                def issue(e):
                    for t in range(4):
                        m = e.transpose(ps[b][:, t * 128:t * 128 + 128], x1[:, t * 128:t * 128 + 128], ident[:])
                    return m
                t = PE.op(issue, l, rest[b])
                tk["ex1"] = t
                tk["kd", p] = rest[b] = AC.op(lambda e: e.activation(
                    kd[p], ps[b][:].rearrange("p (t c) -> p t c", t=4), ACT.Copy), t)

            def updates(p):
                banks, made = [], []
                for odd in range(2):
                    rows = slice(64 * odd, 64 * odd + 64)
                    b = bank()

                    def issue(e, odd=odd, rows=rows, b=b):
                        for n in range(odd, 7, 2):
                            for a in range(2):
                                c = (n // 2) * 128
                                m = e.matmul(ps[b][64 * a:64 * a + 64, c:c + 128],
                                             kd[p][rows, n // 2, a * 64:a * 64 + 64],
                                             vb[rows, n // 2, (2 * p + a) * 128:(2 * p + a) * 128 + 128],
                                             start=True, stop=True)
                        return m
                    banks.append(b)
                    made.append(PE.op(issue, tk["kd", p], tk["vb"], rest[b]))
                for n in range(7):
                    c = (n // 2) * 128
                    u = ps[banks[n % 2]][:, c:c + 128]
                    s = p * 7 + n
                    if n == 0:
                        a = DV.op(lambda e, u=u, s=s: e.tensor_copy(St[:, s, :], u), made)
                    else:
                        a = DV.op(lambda e, u=u, s=s, n=n: e.scalar_tensor_tensor(
                            St[:, s, :], St[:, s - 1, :], dec[:, p * 8 + n:p * 8 + n + 1], u,
                            ALU.mult, ALU.add), a, tk["dec", p])
                    rest[banks[n % 2]] = a
                tk["S", p] = a

            def inner(h):
                p, a = divmod(h, 2)
                rows = slice(64 * a, 64 * a + 64)
                b = bank()

                def issue(e):
                    for t in range(4):
                        c = slice(t * 128, t * 128 + 128)
                        m = e.matmul(ps[b][:, c], ke[p][rows, c], qe[p][rows, c], start=True, stop=True)
                    return m
                t = PE.op(issue, tk["ke", p], tk["qe", p], rest[b])
                s_ = sc[h % 2]
                a_ = AC.op(lambda e: e.activation(s_, ps[b][:].rearrange("p (t c) -> p t c", t=4), ACT.Copy), t,
                           tk.get(("o", h - 2)))
                rest[b] = a_
                m = PL.op(lambda e: e.affine_select(out=s_, in_=s_, compare_op=ALU.is_ge, fill=0.0, base=0,
                                                    pattern=[[0, 4], [1, 128]], channel_multiplier=-1), a_, last_pool())
                tk["sc", h] = PL.op(lambda e: e.memset(s_[0:64, :, 64:128], 0.0), m, last_pool())

            def outer(h):
                p, a = divmod(h, 2)
                rows = slice(64 * a, 64 * a + 64)
                b = bank(hold=True)
                s_ = sc[h % 2]

                def issue(e):
                    for t in range(4):
                        m = e.matmul(ps[b][:, t * 128:t * 128 + 128], vb[:, t, h * 128:h * 128 + 128], s_[:, t, :],
                                     start=(t == 0), stop=(t == 3), skip_group_check=True)
                        for n in (2 * t, 2 * t + 1):
                            if n:
                                m = e.matmul(ps[b][:, n * 64:n * 64 + 64], St[rows, p * 7 + n - 1, :],
                                             qe[p][rows, n * 64:n * 64 + 64], start=False, stop=(n == 7),
                                             skip_group_check=True)
                    return m
                t = PE.op(issue, tk["sc", h], tk["vb"], tk["S", p], rest[b])
                tk["o", h] = t
                tk["sq"] = AC.op(lambda e: e.activation(sq, ps[b][:], ACT.Square), t, tk.get("sq_free"))
                tk["ob", h] = b

            def outer_norm(h):
                b = tk["ob", h]
                b2 = bank()
                m = PE.op(lambda e: e.matmul(ps[b2][:], ones[:], sq, start=True, stop=True), tk["sq"], rest[b2])
                a = AC.op(lambda e: e.activation(rinv, ps[b2][:], ACT.Ln, bias=eps6, scale=1.0 / 128), m, t_eps6,
                          tk.get("rinv_free"))
                rest[b2] = a
                a = AC.op(lambda e: e.activation(rinv, rinv, ACT.Exp, scale=-0.5), a)
                tk["sq_free"] = a
                tk["on", h] = DV.op(lambda e: e.scalar_tensor_tensor(
                    on[:, h, :], ps[b][:], blcol[:, h:h + 1], rinv, ALU.mult, ALU.mult), a, t_sm)
                tk["rinv_free"] = tk["on", h]
                let_go(b, tk["on", h])

            def post_zg(h):
                def post(b, t):
                    s = AC.op(lambda e: e.activation(ub, ps[b][:], ACT.Silu), t, tk.get("ub_free"))
                    rest[b] = s
                    o = DV.op(lambda e: e.tensor_tensor(of, ub, on[:, h, :], ALU.mult), s, tk["on", h],
                              tk.get("of_free"))
                    tk["ub_free"] = o
                    hi = AC.op(lambda e: e.activation(hh[:, 4 + h, :], of, ACT.Copy), o)
                    lo = DV.op(lambda e: e.tensor_tensor(hl[:, 4 + h, :], of, f32(hh[:, 4 + h, :]), ALU.subtract), hi)
                    tk["of_free"] = lo
                    h_ready[4 + h] = [hi, lo]
                return post

            def rows_half(name, dst, act, extra=None):
                banks = {}

                def piece(kb):
                    if kb == 0:
                        for t in range(4):
                            banks[t] = bank(hold=True)
                    j, wh, wl, ready = W.take()
                    for t in range(4):
                        def issue(e, t=t):
                            for k in (0, 1):
                                a = slice(t * 128, t * 128 + 128)
                                m = mm3(e, ps[banks[t]][:], xh[:, 2 * kb + k, a], xl[:, 2 * kb + k, a],
                                        wh[:, k, :], wl[:, k, :], kb + k == 0, 2 * kb + k == 7)
                            return m
                        need = [ready, rest[banks[t]] if kb == 0 else None, x_ready]
                        if kb == 3 or t == 3:
                            tok = PE.op(issue, need)
                        else:
                            PE.quiet(issue, need)
                        if t == 3:
                            W.done(j, tok)
                        if kb == 3:
                            b = banks[t]
                            s = AC.op(lambda e, b=b, t=t: e.activation(dst[:, t, :], ps[b][:], act), tok)
                            let_go(b, s)
                            if extra:
                                s = extra(t, s)
                            tk.setdefault(name, []).append(s)
                return [lambda kb=kb: piece(kb) for kb in range(4)]

            def v_norm(t, ready):
                m = moments(t, 0, v[:, t, :], ready)
                r = inv_std(t, 1, eps6, t_eps6, True, m)
                a = DV.op(lambda e: e.scalar_tensor_tensor(v[:, t, :], v[:, t, :], mv[:, 2 * t:2 * t + 1], lng,
                                                           ALU.subtract, ALU.mult), r, t_ln)
                return DV.op(lambda e: e.scalar_tensor_tensor(v[:, t, :], v[:, t, :], rs[:, t:t + 1], lnb,
                                                              ALU.mult, ALU.add), a)

            def turn_ws():
                b = bank()

                def issue(e):
                    for h in range(4):
                        m = e.transpose(ps[b][:, h * 128:h * 128 + 128], wsb[:, h, :], ident[:])
                    return m
                t = PE.op(issue, t_ws, rest[b])
                a = rest[b] = AC.op(lambda e: e.activation(wT, ps[b][:].rearrange("p (t c) -> p t c", t=4), ACT.Copy), t)
                tk["wT"] = PL.op(lambda e: e.memset(wT[64:128, :, 0:64], 0.0), a, last_pool())

            def mixed(h):
                b = bank()

                def issue(e):
                    e.matmul(ps[b][:].rearrange("p (n i) -> p n i", n=4), ones[0:1, :],
                             bsr[0:1, h * 128:h * 128 + 128].unsqueeze(1).broadcast_to([1, 4, 128]),
                             start=True, stop=True, skip_group_check=True)
                    for t in range(4):
                        m = e.matmul(ps[b][:, t * 128:t * 128 + 128], v[:, t, h * 128:h * 128 + 128], wT[:, h, :],
                                     start=False, stop=True, skip_group_check=True)
                    return m
                tk["mx", h] = (b, PE.op(issue, tk["v"], tk["wT"], t_sm, rest[b]))

            def post_zu(h):
                def post(b, t):
                    s = AC.op(lambda e: e.activation(ub, ps[b][:], ACT.Gelu_apprx_tanh), t, tk.get("ub_free"))
                    rest[b] = s
                    mixed(h)
                    mb, mt = tk["mx", h]
                    o = DV.op(lambda e: e.tensor_tensor(outa[:, h, :], ps[mb][:], ub, ALU.mult), s, mt,
                              tk["o", 3], tk.get("ub_free"))
                    rest[mb] = o
                    tk["ub_free"] = o
                    q = AC.op(lambda e: e.activation([sq, of][h % 2], outa[:, h, :], ACT.Square), o,
                              tk.get(("sqm", h - 2)), tk.get("of_free"), tk.get("sq_free"))
                    if h == 0:
                        tk["rb"] = bank(hold=True)
                    rb = tk["rb"]
                    tk["sqm", h] = PE.op(lambda e: e.matmul(ps[rb][:], ones[:], [sq, of][h % 2], start=(h == 0),
                                                            stop=(h == 3)), q, rest[rb] if h == 0 else None)
                return post

            for f in project(post_zlr):
                f()
            pk = [project(keep(ke[p], ("k", p))) for p in range(2)]
            pq = [project(keep(qe[p], ("q", p), 0.125)) for p in range(2)]
            for f in pk[0]:
                f()
            gate()
            turn_ws()
            for f in pk[1]:
                f()
            for f in pq[0]:
                f()
            cumulate(0)
            cumulate(1)
            for f in pq[1]:
                f()
            for f in rows_half("vb", vb, ACT.Copy):
                f()
            decays(0)
            pv = rows_half("v", v, ACT.Gelu_apprx_tanh, v_norm)
            for f in pv[0:2]:
                f()
            decays(1)
            inner(0)
            inner(1)
            updates(0)
            for f in pv[2:4]:
                f()
            updates(1)
            outer(0)
            fill = []
            for h in range(4):
                fill += project(post_zg(h))
            outer_norm(0)
            order = [lambda: inner(2), lambda: outer(1), lambda: outer_norm(1), lambda: inner(3),
                     lambda: outer(2), lambda: outer_norm(2), lambda: outer(3), lambda: outer_norm(3)]
            at = [1, 1, 2, 5, 5, 6, 9, 10]
            for i, f in enumerate(fill):
                for n, o in zip(at, order):
                    if n == i:
                        o()
                f()
            for h in range(4):
                for f in project(post_zu(h)):
                    f()
            rb = tk["rb"]
            a = AC.op(lambda e: e.activation(rinv, ps[rb][:], ACT.Ln, bias=eps6, scale=1.0 / 512), tk["sqm", 3],
                      tk["rinv_free"])
            let_go(rb, a)
            a = AC.op(lambda e: e.activation(rinv, rinv, ACT.Exp, scale=-0.5), a)
            for h in range(4):
                o = DV.op(lambda e, h=h: e.scalar_tensor_tensor(outa[:, h, :], outa[:, h, :], gocol[:, h:h + 1], rinv,
                                                                ALU.mult, ALU.mult), a)
                hi = AC.op(lambda e, h=h: e.activation(hh[:, h, :], outa[:, h, :], ACT.Copy), o)
                lo = DV.op(lambda e, h=h: e.tensor_tensor(hl[:, h, :], outa[:, h, :], f32(hh[:, h, :]), ALU.subtract), hi)
                h_ready[h] = [hi, lo]

        mixer()
        if upto == 6:
            o = [DV.op(lambda e, k=k: e.tensor_tensor(x[:, k // 2, (k % 2) * 512:(k % 2) * 512 + 512],
                                                     f32(hh[:, k, :]), f32(hl[:, k, :]), ALU.add), h_ready[k])
                 for k in range(8)]
            return finish(nc, locals(), o)

        mb = ar(3072, 4096).rearrange("p (t c) -> p t c", t=4)
        all_h = [h_ready[k] for k in range(8)]
        tg = load_g(0, ap["post_mix_g_2"][0], all_h)
        tp = load_g(2, ap["pre_ff_g_2"][0], all_h)
        fresh = []

        def add_rms(t, m, tg):
            r = inv_std(t, 2, eps6, t_eps6, False, m)
            a = DV.op(lambda e: e.scalar_tensor_tensor(mb[:, t, :], mb[:, t, :], rs[:, t:t + 1], gvec[0],
                                                       ALU.mult, ALU.mult), r, tg)
            last_g[0] = a
            return DV.op(lambda e: e.tensor_tensor(x[:, t, :], x[:, t, :], mb[:, t, :], ALU.add), a)

        def post_w(nh, t, b, token):
            cols = slice(nh * 512, nh * 512 + 512)
            a = rest[b] = AC.op(lambda e: e.activation(mb[:, t, cols], ps[b][:], ACT.Copy), token)
            m = moments(t, nh, mb[:, t, cols], a)
            if nh == 0:
                return None
            return rms_features(t, tp, fresh, add_rms(t, m, tg))

        tokens_out(post_w, hh, hl, lambda k: h_ready[k], 8)
        x_ready[:] = fresh
        if upto == 7:
            return finish(nc, locals(), x_ready)

        rbuf = [ar(7168 + i * 512, 512) for i in range(2)]
        fbuf = [ar(8192 + i * 512, 512) for i in range(2)]
        free, n = {}, [0]
        tg = load_g(0, ap["post_ff_g_2"][0], last_g[0])
        c_out = count("s_out")
        prev = None
        for g in range(4):
            for f in range(8):
                def post(b, t, f=f):
                    i = n[0] % 2
                    s = AC.op(lambda e: e.activation(rbuf[i], ps[b][:], ACT.Relu), t, free.get(n[0] - 2))
                    o = DV.op(lambda e: e.tensor_tensor(fbuf[i], rbuf[i], ps[b][:], ALU.mult), s)
                    rest[b] = o
                    hi = AC.op(lambda e: e.activation(hh[:, f, :], fbuf[i], ACT.Copy), o, prev)
                    lo = DV.op(lambda e: e.tensor_tensor(hl[:, f, :], fbuf[i], f32(hh[:, f, :]), ALU.subtract), hi, prev)
                    h_ready[f] = [hi, lo]
                    free[n[0]] = lo
                    n[0] += 1
                for piece in project(post):
                    piece()

            def post_f(nh, t, b, token, g=g):
                cols = slice(nh * 512, nh * 512 + 512)
                if g == 0:
                    a = AC.op(lambda e: e.activation(mb[:, t, cols], ps[b][:], ACT.Copy), token)
                else:
                    a = DV.op(lambda e: e.tensor_tensor(mb[:, t, cols], mb[:, t, cols], ps[b][:], ALU.add), token)
                rest[b] = a
                if g < 3:
                    return None
                m = moments(t, nh, mb[:, t, cols], a)
                if nh == 0:
                    return None
                a = add_rms(t, m, tg)
                SP.dma(c_out, out[0, t * 128:(t + 1) * 128, :], x[:, t, :], a)
                return None
            tokens_out(post_f, hh, hl, lambda k: h_ready[k], 8)
            prev = W.done_t[W.taken - 1]
        SP.wait((c_out, c_out.value))
        emit(nc, ctx, PE, AC, DV, PL, SP)


def emit(nc, ctx, PE, AC, DV, PL, SP):
    block = ctx.enter_context(nc.Block())
    block.tensor(PE.play)
    block.scalar(AC.play)
    block.vector(DV.play)
    block.gpsimd(PL.play)
    block.sync(SP.play)


def finish(nc, l, tokens):
    SP, x, out = l["SP"], l["x"], l["out"]
    c = l["count"]("s_fin")
    SP.wait(tokens, (l["DV"].count, l["DV"].count.value))
    for t in range(4):
        SP.dma(c, out[0, t * 128:(t + 1) * 128, :], x[:, t, :])
    SP.wait((c, c.value))
    emit(nc, l["ctx"], l["PE"], l["AC"], l["DV"], l["PL"], SP)


def constants():
    inv = (np.float32(10000.0) ** (-np.arange(0, 64, 2, dtype=np.float32) / np.float32(64))).astype(np.float32)
    ang = np.arange(S, dtype=np.float32)[:, None] * inv[None, :]
    cos, sin = np.cos(ang.astype(np.float64)), np.sin(ang.astype(np.float64))
    d = np.arange(128) % 32
    c = cos.T[d].astype(np.float32)
    s = (sin.T[d] * np.where(np.arange(128) < 64, 1.0, -1.0)[:, None]).astype(np.float32)
    m = ((np.arange(128) // 32) % 2).astype(np.float32)
    j, i = np.arange(128)[:, None], np.arange(128)[None, :]
    tri = np.where((j <= i) & (j // 64 == i // 64), np.float32(1 / 16), np.float32(0)).astype(np.float32)
    return {
        "c_ident": np.eye(128, dtype=np.float32), "c_cos": np.ascontiguousarray(c),
        "c_sin": np.ascontiguousarray(s), "c_mask": np.ascontiguousarray(np.stack([1 - m, m], 1)), "c_tri": tri,
    }


def halves_first(w):
    qk = w[..., :2 * D].reshape(D, 16, 2, 2, 32).transpose(0, 1, 3, 2, 4).reshape(1, D, 2 * D)
    return np.concatenate([qk, w[..., 2 * D:]], axis=-1)


_INS = ["x", "a_w_qkv", "a_lambda", "a_subln_g", "a_w_o", "kv_w", "b_w_q", "b_rel_bias", "b_w_o", "ln_g", "ln_b",
        "ffn_w_in", "ffn_w_out", "pre_mix_g_2", "w_in_2", "gmlp_ln_g_2", "gmlp_ln_b_2", "gmlp_ws_2", "gmlp_bs_2",
        "gmlp_out_g_2", "gla_gate_w_2", "gla_gate_b_2", "gla_out_g_2", "w_out_2", "post_mix_g_2", "pre_ff_g_2",
        "w_ff1_2", "w_ff2_2", "post_ff_g_2"]


def kernel(**inputs):
    import concourse.bacc as _bacc
    from concourse.bass_utils import run_bass_kernel_spmd as _run

    nc = _bacc.Bacc("TRN2", target_bir_lowering=False, num_devices=1)
    arrays, aps = {}, {}
    given = {name: np.ascontiguousarray(inputs[name]) for name in _INS}
    given["a_w_qkv"] = halves_first(given["a_w_qkv"])
    given.update(constants())
    for name, a in given.items():
        arrays[f"in_{name}"] = a
        aps[name] = nc.dram_tensor(f"in_{name}", a.shape, mybir.dt.from_np(a.dtype), kind="ExternalInput").ap()
    out = nc.dram_tensor("out_0", (1, S, D), F32, kind="ExternalOutput").ap()
    build(nc, aps, out)
    r = _run(nc, [arrays], core_ids=[0])
    return r.results[0]["out_0"]
```

```python
import math
from contextlib import ExitStack

import numpy as np

import concourse.bass as bass
from concourse import mybir

F32 = mybir.dt.float32
F32R = mybir.dt.float32r
ALU = mybir.AluOpType
ACT = mybir.ActivationFunctionType
AX = mybir.AxisListType.X

D = 1024
S = 512
FF = 2816
FF2 = 4096
NEG = float(np.finfo(np.float32).min)
ALPHA = 4 ** 0.25
LAMBDA_INIT = 0.8 - 0.6 * math.exp(0.0)
ELEN = 640


class Count:

    def __init__(self, sem):
        self.sem, self.value = sem, 0

    def add(self, n):
        self.value += n
        return (self, self.value)


def flat(waits):
    for w in waits:
        if w is None:
            continue
        if isinstance(w, list):
            yield from flat(w)
        else:
            yield w


class Queue:

    def __init__(self, count):
        self.count, self.items, self.waited = count, [], {}

    def wait(self, *tokens):
        for count, value in flat(tokens):
            if self.waited.get(count, 0) < value:
                self.waited[count] = value
                self.items.append(lambda e, c=count, v=value: e.wait_ge(c.sem, v))

    def op(self, issue, *tokens):
        self.wait(*tokens)
        self.items.append(lambda e: issue(e).then_inc(self.count.sem, 1))
        return self.count.add(1)

    def quiet(self, issue, *tokens):
        self.wait(*tokens)
        self.items.append(issue)

    def dma(self, count, out, in_, *tokens, slow=False):
        self.wait(*tokens)
        self.items.append(lambda e: e.dma_start(out, in_, allow_slow_non_contiguous=slow).then_inc(count.sem, 16))
        return count.add(16)

    def play(self, engine):
        for item in self.items:
            item(engine)


def f32(ap):
    return ap.bitcast(F32)


def run_all(items):
    for item in items:
        item()


def weave(main, fill):
    done = 0
    for i, item in enumerate(main):
        upto = len(fill) * (i + 1) // (len(main) + 1)
        while done < upto:
            fill[done]()
            done += 1
        item()
    for item in fill[done:]:
        item()


def build(nc, ap, out, upto=99):
    with ExitStack() as ctx:
        def sb(name, shape, dt=F32):
            return ctx.enter_context(nc.sbuf_tensor(name, shape, dt))

        def count(name):
            return Count(ctx.enter_context(nc.semaphore(name)))

        PE, AC, DV, PL, SP = (Queue(count("s_" + n)) for n in ("pe", "act", "dve", "pool", "sp"))

        ps = [ctx.enter_context(nc.psum_tensor(f"ps{i}", [128, 512], F32)) for i in range(8)]
        RING = 4
        raw = sb("raw", [128, RING, 1024])
        whi = sb("whi", [128, RING, 1024], F32R)
        wlo = sb("wlo", [128, RING, 1024], F32R)
        x = sb("x", [128, 4, D])
        xh = sb("xh", [128, 8, S], F32R)
        xl = sb("xl", [128, 8, S], F32R)
        hh = sb("hh", [128, 8, S], F32R)
        hl = sb("hl", [128, 8, S], F32R)
        arena = sb("arena", [128, 19200])
        ident = sb("ident", [128, 128])
        ones = sb("ones", [128, 128])
        stat = sb("stat", [128, 512])
        small = sb("small", [128, 128])

        def ar(start, n):
            return arena[:, start:start + n]

        rest = [None] * 8
        turn = [0]
        held = set()

        def bank(hold=False):
            while turn[0] % 8 in held:
                turn[0] += 1
            b = turn[0] % 8
            turn[0] += 1
            if hold:
                held.add(b)
            return b

        def let_go(b, token):
            held.discard(b)
            rest[b] = token

        eps5, eps6 = small[:, 0:1], small[:, 1:2]
        nlam, g8 = small[:, 2:3], small[:, 3:4]
        mask0, mask1 = small[:, 4:5], small[:, 5:6]
        gocol, blcol = small[:, 6:10], small[:, 10:14]
        dec = small[:, 16:32]
        bst = small[:, 32:80]
        mv = small[:, 80:88]
        rs = small[:, 88:96]
        lsum = small[:, 96:104]

        c_in = [count(f"s_in{i}") for i in range(12)]
        c_x = [count(f"s_x{i}") for i in range(4)]
        for t in range(4):
            SP.dma(c_x[t], x[:, t, :], ap["x"][0, t * 128:(t + 1) * 128, :])
            xw0 = None
        t_ident = SP.dma(c_in[0], ident[:], ap["c_ident"])
        x_in = [(c_x[t], 16) for t in range(4)]

        def last_pool():
            return (PL.count, PL.count.value)

        t_ones = PL.op(lambda e: e.memset(ones[:], 1.0))
        t_eps5 = PL.op(lambda e: e.memset(eps5, 1e-5), last_pool())
        t_eps6 = PL.op(lambda e: e.memset(eps6, 1e-6), last_pool())

        plan = []

        def plan_cols(w, c0, n=8, k0=0):
            plan.append((w[k0 * 128:(k0 + n) * 128, c0:c0 + 128], n, 128))

        def plan_rows(w, k0, c0):
            plan.append((w[k0 * 128:(k0 + 2) * 128, c0:c0 + 512], 2, 512))

        def plan_out(w, k0, nk):
            for nh in range(2):
                for k in range(k0, k0 + nk, 2):
                    plan_rows(w, k, nh * 512)

        qkv, kvw, bq = ap["a_w_qkv"][0], ap["kv_w"], ap["b_w_q"][0]
        win2 = ap["w_in_2"][0]
        groups = [(0, 8), (8, 8), (16, 6)]
        for nh in range(2):
            for k in range(0, 8, 2):
                plan_rows(qkv, k, 2048 + nh * 512)
        for h in range(8):
            plan_cols(qkv, h * 128)
            plan_cols(qkv, 1024 + h * 128)
        plan_out(ap["a_w_o"][0], 0, 8)

        def plan_ffn(layer):
            for f0, nf in groups:
                for f in range(f0, f0 + nf):
                    plan_cols(ap["ffn_w_in"][layer], f * 128)
                    plan_cols(ap["ffn_w_in"][layer], FF + f * 128)
                plan_out(ap["ffn_w_out"][layer], f0, nf)

        plan_ffn(0)
        for nh in range(2):
            for k in range(0, 8, 2):
                plan_rows(kvw, k, 1024 + nh * 512)
        for p in range(8):
            plan_cols(bq, p * 128)
            plan_cols(kvw, p * 128)
        plan_out(ap["b_w_o"][0], 0, 8)
        plan_ffn(1)
        zlr_at = len(plan)
        plan_cols(win2, 2448)
        for c in (1280, 1408, 1024, 1152):
            plan_cols(win2, c)
        for c in (1536, 512):
            for k in range(0, 8, 2):
                plan_rows(win2, k, c)
        for c in range(4):
            plan_cols(win2, 2048 + c * 128)
        for c in range(4):
            plan_cols(win2, c * 128)
        plan_out(ap["w_out_2"][0], 0, 8)
        for g in range(4):
            for f in range(8):
                plan_cols(ap["w_ff1_2"][0], (g * 8 + f) * 128)
            plan_out(ap["w_ff2_2"][0], g * 8, 8)

        class Weights:
            def __init__(self):
                self.c = [count(f"s_w{i}") for i in range(RING)]
                self.loaded, self.split_n, self.taken = 0, 0, 0
                self.dma_t, self.hi_t, self.lo_t, self.done_t = {}, {}, {}, {}
                while self.loaded < RING:
                    self.load()

            def load(self):
                j = self.loaded
                if j >= len(plan):
                    return
                src, n, cols = plan[j]
                s = j % RING
                dst = raw[:, s, :].rearrange("p (k c) -> p k c", k=n)
                free = [self.hi_t.get(j - RING), self.lo_t.get(j - RING)]
                if j == zlr_at:
                    view = win2.rearrange("(k p) c -> p k c", p=128)
                    SP.dma(self.c[s], dst[:, :, 0:16], view[:, :, 2560:2576], free)
                    t = SP.dma(self.c[s], dst[:, :, 16:128], view[:, :, 2448:2560])
                else:
                    t = SP.dma(self.c[s], dst, src.rearrange("(k p) c -> p k c", p=128), free)
                self.dma_t[j] = t
                self.loaded += 1

            def pump(self):
                while self.split_n < min(len(plan), self.taken + RING - 1):
                    j = self.split_n
                    if j >= RING and j - RING not in self.done_t:
                        return
                    s = j % RING
                    free = self.done_t.get(j - RING)
                    self.hi_t[j] = AC.op(lambda e, s=s: e.activation(whi[:, s, :], raw[:, s, :], ACT.Copy),
                                         self.dma_t[j], free)
                    self.lo_t[j] = DV.op(lambda e, s=s: e.tensor_tensor(wlo[:, s, :], raw[:, s, :],
                                                                        f32(whi[:, s, :]), ALU.subtract),
                                         self.dma_t[j], self.hi_t[j], free)
                    self.split_n += 1
                    self.load()

            def take(self):
                j = self.taken
                self.taken += 1
                self.pump()
                assert j < self.split_n
                _, n, cols = plan[j]
                s = j % RING
                h = whi[:, s, :].rearrange("p (k c) -> p k c", k=n)
                low = wlo[:, s, :].rearrange("p (k c) -> p k c", k=n)
                return j, h, low, [self.hi_t[j], self.lo_t[j]]

            def done(self, j, token):
                self.done_t[j] = token
                self.pump()

        def table(name):
            AC.quiet(lambda e: e.preload_act_table_set(name))

        W = Weights()
        table("natural_log_exp_and_others")
        W.pump()

        def mm3(e, o, ah, al, bh, bl, start, stop):
            e.matmul(o, ah, bh, start=start, stop=False)
            e.matmul(o, ah, bl, start=False, stop=False)
            return e.matmul(o, al, bh, start=False, stop=stop)

        x_ready = []
        x_tile = [None] * 4
        h_ready = [None] * 8

        def project(post):
            st = {}

            def piece(i):
                if i == 0:
                    st["w"] = W.take()
                    st["b"] = bank(hold=True)
                j, wh, wl, ready = st["w"]
                b = st["b"]

                def issue(e):
                    for k in (2 * i, 2 * i + 1):
                        m = mm3(e, ps[b][:], wh[:, k, :], wl[:, k, :], xh[:, k, :], xl[:, k, :], k == 0, k == 7)
                    return m

                if i < 3:
                    PE.quiet(issue, *([ready, rest[b], x_ready] if i == 0 else []))
                else:
                    t = PE.op(issue)
                    W.done(j, t)
                    held.discard(b)
                    post(b, t)

            return [lambda i=i: piece(i) for i in range(4)]

        def tokens_out(post, ah, al, ready_of, nk):
            later, st, pieces = [], {}, []

            def piece(nh, blocks, n, t):
                k0 = blocks[n]
                if k0 == 0 and t == 0:
                    st["b"] = [bank(hold=True) for _ in range(4)]
                if t == 0:
                    st[n] = W.take()
                j, wh, wl, ready = st[n]
                b = st["b"][t]

                def issue(e):
                    for k in (0, 1):
                        a = slice(t * 128, t * 128 + 128)
                        m = mm3(e, ps[b][:], ah[:, k0 + k, a], al[:, k0 + k, a],
                                wh[:, k, :], wl[:, k, :], k0 + k == 0, k0 + k == nk - 1)
                    return m
                need = [ready, rest[b] if k0 == 0 else None, ready_of(k0, t), ready_of(k0 + 1, t)]
                if t < 3 and k0 < nk - 2:
                    PE.quiet(issue, need)
                    return
                token = PE.op(issue, need)
                if t == 3:
                    W.done(j, token)
                if k0 == nk - 2:
                    held.discard(b)
                    while later:
                        later.pop()()
                    more = post(nh, t, b, token)
                    if more:
                        later.append(more)

            for nh in range(2):
                blocks = list(range(0, nk, 2))
                n_tiled = min(3, len(blocks))
                if nh == 0:
                    runs = [blocks[:n_tiled]] + [[k] for k in blocks[n_tiled:]]
                else:
                    runs = [[k] for k in blocks[:-n_tiled]] + [blocks[-n_tiled:]]
                for run in runs:
                    for t in range(4):
                        for n in range(len(run)):
                            pieces.append(lambda nh=nh, run=run, n=n, t=t: piece(nh, run, n, t))

            def rest_of():
                while later:
                    later.pop()()
            pieces.append(rest_of)
            return pieces

        def to_features(t, src, ready):
            tokens = []
            for half in range(2):
                b = bank()

                def issue(e, half=half, b=b):
                    for k in range(4):
                        m = e.transpose(ps[b][:, k * 128:(k + 1) * 128],
                                        src[:, (half * 4 + k) * 128:(half * 4 + k + 1) * 128], ident[:])
                    return m
                tr = PE.op(issue, ready, rest[b], t_ident)
                dst = (slice(None), slice(half * 4, half * 4 + 4), slice(t * 128, t * 128 + 128))
                view = ps[b][:].rearrange("p (k c) -> p k c", k=4)
                hi = AC.op(lambda e, dst=dst, view=view: e.activation(xh[dst], view, ACT.Copy), tr)
                lo = DV.op(lambda e, dst=dst, view=view: e.tensor_tensor(xl[dst], view, f32(xh[dst]), ALU.subtract), hi)
                rest[b] = lo
                tokens += [hi, lo]
            x_tile[t] = tokens
            return tokens

        def moments(t, part, src, ready):
            return DV.op(lambda e: e.bn_stats(bst[:, t * 12 + part * 6:t * 12 + part * 6 + 6], src), ready)

        def inv_std(t, parts, eps, t_eps, plain, ready):
            m, r = mv[:, 2 * t:2 * t + 2], rs[:, t:t + 1]
            a = DV.op(lambda e: e.bn_aggr(m, bst[:, t * 12:t * 12 + 6 * parts]), ready)
            if not plain:
                a = DV.op(lambda e: e.scalar_tensor_tensor(m[:, 1:2], m[:, 0:1], m[:, 0:1], m[:, 1:2],
                                                           ALU.mult, ALU.add), a)
            s = AC.op(lambda e: e.activation(lsum[:, t:t + 1], m[:, 1:2], ACT.Sqrt, bias=eps), a, t_eps)
            return DV.op(lambda e: e.reciprocal(r, lsum[:, t:t + 1]), s)

        gvec = [ar(i * 1024, 1024) for i in range(3)]
        c_g = [count(f"s_g{i}") for i in range(3)]

        def load_g(i, v, *free):
            src = bass.AP(tensor=v.tensor, offset=v.offset, ap=[[0, 128], [1, 1024]])
            return SP.dma(c_g[i], gvec[i], src, *free)

        last_g = [None, None, None]

        def layer_norm(t, ready, tg, tb):
            r = inv_std(t, 2, eps5, t_eps5, True, ready)
            a = DV.op(lambda e: e.scalar_tensor_tensor(x[:, t, :], x[:, t, :], mv[:, 2 * t:2 * t + 1], gvec[0],
                                                       ALU.subtract, ALU.mult), r, tg)
            a = DV.op(lambda e: e.scalar_tensor_tensor(x[:, t, :], x[:, t, :], rs[:, t:t + 1], gvec[1],
                                                       ALU.mult, ALU.add), a, tb)
            return a

        def residual_norm(i, last_group=True, first_group=True, after=None, vecs=None):
            first = {}
            ready = []

            def post(nh, t, b, token):
                cols = slice(nh * 512, nh * 512 + 512)
                scale = ALPHA if first_group else 1.0
                a = DV.op(lambda e: e.scalar_tensor_tensor(x[:, t, cols], x[:, t, cols], scale, ps[b][:],
                                                           ALU.mult, ALU.add), token)
                rest[b] = a
                if not last_group:
                    return None
                m = moments(t, nh, x[:, t, cols], a)
                if nh == 0:
                    return None
                return after(t, m)
            return post

        def norm_then_features(ln, row):
            l, r = divmod(row, 2)
            tg = load_g(0, ap["ln_g"][l, r], last_g[0])
            tb = load_g(1, ap["ln_b"][l, r], last_g[1])
            fresh = []

            def after(t, m):
                a = layer_norm(t, m, tg, tb)
                last_g[0] = last_g[1] = a

                def pe():
                    fresh.extend(to_features(t, x[:, t, :], a))
                return pe
            return after, fresh

        for t in range(4):
            x_ready += to_features(t, x[:, t, :], x_in[t])

        BASE = 3072

        def values_out(base, V):
            tokens = []

            def post(nh, t, b, token):
                a = AC.op(lambda e: e.activation(V[:, t, nh * 512:nh * 512 + 512], ps[b][:], ACT.Copy), token)
                rest[b] = a
                tokens.append(a)
                return None
            return tokens, tokens_out(post, xh, xl, lambda k, t: x_tile[t] or x_ready, 8)

        esb = ar(BASE + 15360, 640)
        e2 = nc.dram_tensor("bias_rows", [16, ELEN], F32, kind="Internal").ap()
        toep = nc.dram_tensor("bias_skewed", [16, 128 * ELEN], F32, kind="Internal").ap()
        c_b = [count(f"s_b{i}") for i in range(5)]
        rel = ap["b_rel_bias"][0]
        t_toep = []

        def bias_rows():
            t1 = SP.dma(c_b[0], esb[0:16, 256:640], rel[:, 1:385])
            t2 = SP.dma(c_b[0], esb[0:16, 0:2], rel[:, 0:2])
            t3 = PL.op(lambda e: e.tensor_copy(esb[0:16, 1:256], esb[0:16, 0:1].broadcast_to([16, 255])), t1, t2,
                       last_pool())
            return SP.dma(c_b[1], e2, esb[0:16, :], t3)

        def bias_skewed(h, n, ready):
            src = bass.AP(tensor=e2.tensor, offset=h * ELEN, ap=[[ELEN, n], [0, 128], [1, ELEN]])
            dst = bass.AP(tensor=toep.tensor, offset=h * 128 * ELEN, ap=[[128 * ELEN, n], [ELEN, 128], [1, ELEN]])
            t_toep.append(SP.dma(c_b[2], dst, src, ready))

        AHEAD_A = 8
        ORDER_A = "S0 - t3 - S1 F0 w F1 T0 S2 - - F2 T1 S3 - - F3 T2 n -".split()

        def attention_a(then):
            cosb, sinb = ar(BASE, 512), ar(BASE + 512, 512)
            qk = [[ar(BASE + 1024 + (n * 3 + i) * 512, 512) for i in range(3)] for n in range(2)]
            qk.append([ar(BASE + 13824 + i * 512, 512) for i in range(3)])
            V = ar(BASE + 4096, 4096).rearrange("p (t c) -> p t c", t=4)
            ebuf = [[ar(BASE + 8192 + (n * 2 + m) * 512, 512) for m in range(2)] for n in range(2)]
            aT = ar(BASE + 10240, 2048).rearrange("p (j q) -> p j q", j=4)
            tmp, sq, of = (ar(BASE + 12288 + i * 512, 512) for i in range(3))
            lam4 = ar(BASE + 12288, 256)
            t_cos = SP.dma(c_in[1], cosb, ap["c_cos"])
            t_sin = SP.dma(c_in[1], sinb, ap["c_sin"])
            t_mask = SP.dma(c_in[2], small[:, 4:6], ap["c_mask"])
            t_sub = SP.dma(c_in[3], g8, ap["a_subln_g"][0].rearrange("(p a) -> p a", a=1), slow=True)
            lp = ap["a_lambda"][0]
            t_lam = SP.dma(c_in[4], lam4, bass.AP(tensor=lp.tensor, offset=lp.offset, ap=[[0, 128], [1, 256]]))
            v_ready, pieces = values_out(0, V)
            run_all(pieces)
            t_g8 = DV.op(lambda e: e.tensor_scalar(g8, g8, 1.0 - LAMBDA_INIT, None, ALU.mult), t_sub)
            l1 = DV.op(lambda e: e.tensor_tensor_reduce(sq[:, 0:64], lam4[:, 0:64], lam4[:, 64:128], 1.0, 0.0,
                                                        ALU.mult, ALU.add, lsum[:, 0:1]), t_lam)
            l2 = DV.op(lambda e: e.tensor_tensor_reduce(sq[:, 64:128], lam4[:, 128:192], lam4[:, 192:256], 1.0, 0.0,
                                                        ALU.mult, ALU.add, lsum[:, 1:2]), t_lam)
            le = AC.op(lambda e: e.activation(lsum[:, 2:4], lsum[:, 0:2], ACT.Exp), l1, l2)
            l3 = DV.op(lambda e: e.tensor_tensor(nlam, lsum[:, 3:4], lsum[:, 2:3], ALU.subtract), le)
            t_nlam = DV.op(lambda e: e.tensor_scalar(nlam, nlam, -LAMBDA_INIT, None, ALU.add), l3)

            t_rows = bias_rows()
            qk_ready = {}
            qk_free = {}

            tmp_free = [None]

            def rope(h, which):
                def post(b, t):
                    q0, q1, k = qk[h % 3]
                    dst = k if which else q0
                    u0 = DV.op(lambda e: e.tensor_tensor(tmp[0:64, :], ps[b][64:128, :], sinb[64:128, :], ALU.mult),
                               t, t_sin, t_nlam, tmp_free[0])
                    u1 = DV.op(lambda e: e.tensor_tensor(tmp[64:128, :], ps[b][0:64, :], sinb[0:64, :], ALU.mult))
                    a = rest[b] = DV.op(lambda e: e.tensor_tensor(dst, ps[b][:], cosb, ALU.mult), t_cos,
                                        qk_free.get(h - 3))
                    s = tmp_free[0] = PL.op(lambda e: e.tensor_tensor(dst, dst, tmp, ALU.add), a, u0, u1,
                                            last_pool())
                    if not which:
                        q1t = PL.op(lambda e: e.tensor_scalar(q1, q0, mask1, None, ALU.mult), s, t_mask)
                        s = PL.op(lambda e: e.tensor_scalar(q0, q0, mask0, None, ALU.mult), q1t)
                    qk_ready.setdefault(h, []).append(s)
                return post

            a_ready, tr_done, at_ready, exp_done = {}, {}, {}, {}

            def scores(h, i):
                q0, q1, k = qk[h % 3]
                n = (i + 1) * 128
                c = (h * 4 + i) * 8
                mx, nb = stat[:, c:c + 2], stat[:, c + 2:c + 4]
                ls, r = stat[:, c + 4:c + 6], stat[:, c + 6:c + 8]
                buf = (h * 4 + i) % 2
                maxes, banks = [], []
                for m, q in enumerate((q0, q1)):
                    b = bank()
                    banks.append(b)
                    t = PE.op(lambda e, q=q, b=b: e.matmul(ps[b][:, 0:n], q[:, i * 128:i * 128 + 128], k[:, 0:n],
                                                           start=True, stop=True), qk_ready[h], rest[b])
                    qk_free[h] = t
                    t = DV.op(lambda e, b=b: e.memset(ps[b][0:64, n - 64:n], NEG), t)
                    maxes.append(DV.op(lambda e, b=b, m=m: e.reduce_max(mx[:, m:m + 1], ps[b][:, 0:n], AX), t))
                t = DV.op(lambda e: e.tensor_scalar(nb, mx, -0.125, None, ALU.mult), maxes)
                exps = []
                for m in range(2):
                    b = banks[m]
                    exps.append(AC.op(lambda e, m=m, b=b: e.activation(
                        ebuf[buf][m][:, 0:n], ps[b][:, 0:n], ACT.Exp, bias=nb[:, m:m + 1], scale=0.125,
                        accum_out=ls[:, m:m + 1]), t, tr_done.get((h * 4 + i) - 2)))
                    rest[b] = exps[-1]
                exp_done[h, i] = exps

            def shares(h, i):
                n = (i + 1) * 128
                c = (h * 4 + i) * 8
                ls, r = stat[:, c + 4:c + 6], stat[:, c + 6:c + 8]
                buf = (h * 4 + i) % 2
                t = DV.op(lambda e: e.reciprocal(r, ls), exp_done[h, i])
                r1 = DV.op(lambda e: e.tensor_tensor(r[:, 1:2], r[:, 1:2], nlam, ALU.mult), t, t_nlam)
                e0, e1 = ebuf[buf][0][:, 0:n], ebuf[buf][1][:, 0:n]
                t = DV.op(lambda e: e.tensor_scalar(e0, e0, r[:, 0:1], None, ALU.mult), t)
                a_ready[h, i] = DV.op(lambda e: e.scalar_tensor_tensor(e0, e1, r[:, 1:2], e0, ALU.mult, ALU.add), t, r1)

            def turn_over(h, i):
                buf = (h * 4 + i) % 2
                e0 = ebuf[buf][0]
                b = bank()

                def issue(e):
                    for j in range(i + 1):
                        m = e.transpose(ps[b][:, j * 128:j * 128 + 128], e0[:, j * 128:j * 128 + 128], ident[:])
                    return m
                t = PE.op(issue, a_ready[h, i], rest[b])
                tr_done[h * 4 + i] = t
                n = (i + 1) * 128
                a = AC.op(lambda e: e.activation(aT[:, 0:i + 1, i * 128:i * 128 + 128],
                                                 ps[b][:, 0:n].rearrange("p (j q) -> p j q", j=i + 1), ACT.Copy), t)
                rest[b] = a
                at_ready[h, i] = a

            sq_free = [None]

            def weigh(h):
                b = bank(hold=True)

                def issue(e):
                    for j in range(4):
                        m = e.matmul(ps[b][:, j * 128:512], V[:, j, h * 128:h * 128 + 128], aT[:, j, j * 128:512],
                                     start=(j == 0), stop=(j == 3))
                    return m
                t = PE.op(issue, v_ready, rest[b], [at_ready[h, i] for i in range(4)])
                st[h] = (b, AC.op(lambda e: e.activation(sq, ps[b][:], ACT.Square), t, l1, l2, sq_free[0]))

            st = {}

            def norm(h):
                b, t = st[h]
                b2 = bank()
                m = PE.op(lambda e: e.matmul(ps[b2][:], ones[:], sq, start=True, stop=True), t, rest[b2], t_ones)
                a = AC.op(lambda e: e.activation(sq, ps[b2][:], ACT.Ln, bias=eps5, scale=1.0 / 128), m, t_eps5)
                rest[b2] = a
                a = AC.op(lambda e: e.activation(sq, sq, ACT.Exp, scale=-0.5), a)
                o = DV.op(lambda e: e.scalar_tensor_tensor(of, ps[b][:], g8, sq, ALU.mult, ALU.mult), a, t_g8,
                          h_ready[h - 1] if h else None)
                let_go(b, o)
                sq_free[0] = o
                hi = AC.op(lambda e: e.activation(hh[:, h, :], of, ACT.Copy), o)
                lo = DV.op(lambda e: e.tensor_tensor(hl[:, h, :], of, f32(hh[:, h, :]), ALU.subtract), hi)
                h_ready[h] = [hi, lo]

            def proj(h):
                return project(rope(h, 0)) + project(rope(h, 1))

            run_all(proj(0))
            fill = [f for h in range(1, 8) for f in proj(h)] + then[:12]
            run_all(fill[:AHEAD_A])
            fill = iter(fill[AHEAD_A:])
            steps = {"S": scores, "F": shares, "T": turn_over}
            for h in range(9):
                if h < 8:
                    bias_skewed(2 * h, 2, t_rows)
                for step in ORDER_A:
                    if step == "-":
                        f = next(fill, None)
                        if f:
                            f()
                        continue
                    g = h - step[0].islower()
                    if not 0 <= g < 8:
                        continue
                    if step == "w":
                        weigh(g)
                    elif step == "n":
                        norm(g)
                    else:
                        steps[step[0].upper()](g, int(step[1]))
            run_all(fill)

        def ffn(layer, after_row, tail):
            sbuf_ = [ar(BASE + i * 512, 512) for i in range(2)]
            hbuf = [ar(BASE + 1024 + i * 512, 512) for i in range(2)]
            s_free, n = {}, [0]
            w_tail, fresh = None, None
            for gi, (f0, nf) in enumerate(groups):
                for f in range(nf):
                    st = {}

                    def post_gate(b, t, f=f):
                        i = n[0] % 2
                        st["s"] = AC.op(lambda e: e.activation(sbuf_[i], ps[b][:], ACT.Silu), t, s_free.get(n[0] - 2))
                        rest[b] = st["s"]

                    def post_up(b, t, f=f):
                        i = n[0] % 2
                        o = DV.op(lambda e: e.tensor_tensor(hbuf[i], ps[b][:], sbuf_[i], ALU.mult), t, st["s"],
                                  s_free.get(n[0] - 2))
                        rest[b] = o
                        hi = AC.op(lambda e: e.activation(hh[:, f, :], hbuf[i], ACT.Copy), o)
                        lo = DV.op(lambda e: e.tensor_tensor(hl[:, f, :], hbuf[i], f32(hh[:, f, :]), ALU.subtract), hi)
                        h_ready[f] = [hi, lo]
                        s_free[n[0]] = lo
                        n[0] += 1
                    if gi:
                        AC.wait(prev)
                        DV.wait(prev)
                    for piece in project(post_gate) + project(post_up):
                        piece()
                last = gi == len(groups) - 1
                if last:
                    after, fresh = tail(after_row)
                post = residual_norm(0, last, gi == 0, after if last else None)
                run_all(tokens_out(post, hh, hl, lambda k, t: h_ready[k], nf))
                prev = W.done_t[W.taken - 1]
            x_ready[:] = fresh

        after, fresh = norm_then_features(0, 0)
        pieces = tokens_out(residual_norm(0, True, True, after), hh, hl, lambda k, t: h_ready[k], 8)
        attention_a(pieces)
        run_all(pieces[12:])
        x_ready[:] = fresh
        if upto == 2:
            return finish(nc, locals(), x_ready)
        ffn(0, 1, lambda row: norm_then_features(0, row))
        if upto == 3:
            return finish(nc, locals(), x_ready)

        AHEAD_B = 4
        ORDER_B = "S00 - t13 S01 F00 w S02 F01 T00 - S03 F02 T01 - S10 F03 T02 - S11 F10 T03 - S12 F11 T10 - S13 F12 T11 - F13 T12 -".split()

        def attention_b(then):
            table("natural_log_exp_and_others")
            qk = [[ar(BASE + (n * 2 + i) * 512, 512) for i in range(2)] for n in range(2)]
            qk.append([ar(BASE + 12288 + i * 512, 512) for i in range(2)])
            V = ar(BASE + 4096, 4096).rearrange("p (t c) -> p t c", t=4)
            ebuf = [ar(BASE + 8192 + n * 512, 512) for n in range(3)]
            PT = [ar(BASE + c, 2048).rearrange("p (j q) -> p j q", j=4) for c in (10240, 13312)]
            bt = [ar(BASE + 2048 + n * 512, 512) for n in range(3)]
            v_ready, pieces = values_out(0, V)
            run_all(pieces)
            qk_ready, qk_free = {}, {}
            bt_ready, bt_free = {}, {}

            def load_bias(h):
                i = h % 3
                src = bass.AP(tensor=toep.tensor, offset=h * 128 * ELEN + 127, ap=[[ELEN - 1, 128], [1, 512]])
                t = SP.dma(c_b[3 + i] if i < 2 else c_b[0], bt[i], src, t_toep[-1], bt_free.get(h - 3), v_ready)
                bt_ready[h] = PL.op(lambda e: e.memset(bt[i][0:64, 448:512], NEG), t, last_pool())

            def keep(p, which):
                def post(b, t):
                    if which:
                        s = AC.op(lambda e: e.activation(qk[p % 3][1], ps[b][:], ACT.Copy), t, qk_free.get(p - 3))
                    else:
                        s = AC.op(lambda e: e.activation(qk[p % 3][0], ps[b][:], ACT.Copy, scale=0.125), t,
                                  qk_free.get(p - 3))
                    rest[b] = s
                    qk_ready.setdefault(p, []).append(s)
                return post

            p_ready, tr_done, pt_ready, exp_done = {}, {}, {}, {}

            def scores(h, i):
                p, a = divmod(h, 2)
                q, k = qk[p % 3]
                n = (i + 1) * 128
                c = (h * 4 + i) * 4
                mx, nb, ls = (stat[:, c + z:c + z + 1] for z in range(3))
                s = h * 4 + i
                e_ = ebuf[s % 3][:, 0:n]
                rows = slice(64 * a, 64 * a + 64)
                b = bank()
                t = PE.op(lambda e: e.matmul(ps[b][:, 0:n], q[rows, i * 128:i * 128 + 128], k[rows, 0:n],
                                             start=True, stop=True), qk_ready[p], rest[b])
                qk_free[p] = t
                t = DV.op(lambda e: e.tensor_tensor_reduce(e_, ps[b][:, 0:n], bt[h % 3][:, 384 - 128 * i:512], 1.0, NEG,
                                                           ALU.add, ALU.max, mx), t, bt_ready[h], tr_done.get(s - 3))
                rest[b] = t
                bt_free[h] = t
                t = DV.op(lambda e: e.tensor_scalar(nb, mx, -1.0, None, ALU.mult), t)
                exp_done[s] = AC.op(lambda e: e.activation(e_, e_, ACT.Exp, bias=nb, accum_out=ls), t)

            def shares(h, i):
                c = (h * 4 + i) * 4
                ls, r = stat[:, c + 2:c + 3], stat[:, c + 3:c + 4]
                s = h * 4 + i
                e_ = ebuf[s % 3][:, 0:(i + 1) * 128]
                t = DV.op(lambda e: e.reciprocal(r, ls), exp_done[s])
                p_ready[s] = DV.op(lambda e: e.tensor_scalar(e_, e_, r, None, ALU.mult), t)

            def turn_over(h, i):
                s = h * 4 + i
                e_ = ebuf[s % 3]
                b = bank()

                def issue(e):
                    for j in range(i + 1):
                        m = e.transpose(ps[b][:, j * 128:j * 128 + 128], e_[:, j * 128:j * 128 + 128], ident[:])
                    return m
                t = PE.op(issue, p_ready[s], rest[b])
                tr_done[s] = t
                n = (i + 1) * 128
                pt_ready[h, i] = rest[b] = AC.op(lambda e: e.activation(
                    PT[h % 2][:, 0:i + 1, i * 128:i * 128 + 128],
                    ps[b][:, 0:n].rearrange("p (j q) -> p j q", j=i + 1), ACT.Copy), t)

            def weigh(p):
                b = bank(hold=True)

                def issue(e):
                    for j in range(4):
                        for a in range(2):
                            h = 2 * p + a
                            m = e.matmul(ps[b][64 * a:64 * a + 64, j * 128:512], V[:, j, h * 64:h * 64 + 64],
                                         PT[a][:, j, j * 128:512], start=(j == 0), stop=(j == 3))
                    return m
                t = PE.op(issue, v_ready, rest[b], [pt_ready[2 * p + a, i] for a in range(2) for i in range(4)])
                hi = AC.op(lambda e: e.activation(hh[:, p, :], ps[b][:], ACT.Copy), t)
                lo = DV.op(lambda e: e.tensor_tensor(hl[:, p, :], ps[b][:], f32(hh[:, p, :]), ALU.subtract), hi)
                let_go(b, lo)
                h_ready[p] = [hi, lo]

            def proj(p):
                return project(keep(p, 0)) + project(keep(p, 1))

            load_bias(0)
            load_bias(1)
            run_all(proj(0))
            fill = [f for p in range(1, 8) for f in proj(p)] + then[:12]
            run_all(fill[:AHEAD_B])
            fill = iter(fill[AHEAD_B:])
            steps = {"S": scores, "F": shares, "T": turn_over}
            for p in range(9):
                for step in ORDER_B:
                    if step == "-":
                        f = next(fill, None)
                        if f:
                            f()
                        continue
                    g = p - step[0].islower()
                    if not 0 <= g < 8:
                        continue
                    if step == "w":
                        weigh(g)
                        continue
                    h, i = 2 * g + int(step[1]), int(step[2])
                    if step[0] == "S" and i == 2 and h + 2 < 16:
                        load_bias(h + 2)
                    steps[step[0].upper()](h, i)
            run_all(fill)

        after, fresh = norm_then_features(1, 2)
        pieces = tokens_out(residual_norm(0, True, True, after), hh, hl, lambda k, t: h_ready[k], 8)
        attention_b(pieces)
        run_all(pieces[12:])
        x_ready[:] = fresh

        yb = [ar(9216 + i * 1024, 1024) for i in range(2)]
        y_free = [None, None]

        def rms_features(t, tg, fresh, ready):
            m0 = moments(t, 0, x[:, t, 0:512], ready)
            m1 = moments(t, 1, x[:, t, 512:1024], ready)
            r = inv_std(t, 2, eps6, t_eps6, False, [m0, m1])
            y = yb[t % 2]
            a = DV.op(lambda e: e.scalar_tensor_tensor(y, x[:, t, :], rs[:, t:t + 1], gvec[2], ALU.mult, ALU.mult),
                      r, tg, y_free[t % 2])
            last_g[2] = a

            def pe():
                fresh.extend(to_features(t, y, a))
                y_free[t % 2] = (PE.count, PE.count.value)
            return pe

        def tail_two(row):
            l, r_ = divmod(row, 2)
            tg = load_g(0, ap["ln_g"][l, r_], last_g[0])
            tb = load_g(1, ap["ln_b"][l, r_], last_g[1])
            tp = load_g(2, ap["pre_mix_g_2"][0], last_g[2])
            fresh = []

            def after(t, m):
                a = layer_norm(t, m, tg, tb)
                last_g[0] = last_g[1] = a
                return rms_features(t, tp, fresh, a)
            return after, fresh
        ffn(1, 3, tail_two)
        if upto == 5:
            return finish(nc, locals(), x_ready)

        def mixer():
            v = ar(3072, 2048).rearrange("p (t c) -> p t c", t=4)
            vb = ar(5120, 2048).rearrange("p (t c) -> p t c", t=4)
            qe = [ar(7168 + p * 512, 512) for p in range(2)]
            ke = [ar(8192 + p * 512, 512) for p in range(2)]
            outa = ar(7168, 2048).rearrange("p (h q) -> p h q", h=4)
            la = ar(9216, 1024).rearrange("p (t c) -> p t c", t=4)
            cum = [ar(10240, 512), ar(10752, 512)]
            on = ar(9216, 2048).rearrange("p (h q) -> p h q", h=4)
            ex = [ar(11264, 512), ar(11776, 512)]
            sc = [ar(12288 + i * 512, 512).rearrange("p (t c) -> p t c", t=4) for i in range(2)]
            wT = ar(13312, 512).rearrange("p (h i) -> p h i", h=4)
            sq, rinv, of, ub = (ar(13824 + i * 512, 512) for i in range(4))
            wsb = ar(15872, 512).rearrange("p (h j) -> p h j", h=4)
            bsr = ar(16384, 512)
            gw, gb = ar(16896, 256), ar(17152, 512)
            zl = ar(17664, 512)
            lng, lnb = ar(18176, 512), ar(18688, 512)
            kd = [ar(p * 512, 512).rearrange("p (t c) -> p t c", t=4) for p in range(2)]
            St = ar(1024, 1792).rearrange("p (n c) -> p n c", n=14)
            tri = sb("tri", [128, 128])
            t_tri = SP.dma(c_in[5], tri[:], ap["c_tri"])
            wide = lambda u, n: bass.AP(tensor=u.tensor, offset=u.offset, ap=[[0, 128], [1, n]])
            SP.wait(x_ready)
            t_ws = SP.dma(c_in[6], wsb, ap["gmlp_ws_2"][0].rearrange("h i j -> i h j"))
            SP.dma(c_in[7], bsr[0:1, :], ap["gmlp_bs_2"].rearrange("a h i -> a (h i)"))
            SP.dma(c_in[7], gw[0:16, :], ap["gla_gate_w_2"][0])
            SP.dma(c_in[7], gb[0:1, 0:256], ap["gla_gate_b_2"])
            SP.dma(c_in[7], gb[0:1, 256:512], ap["gla_gate_b_2"])
            SP.dma(c_in[7], gocol, ap["gmlp_out_g_2"][0].rearrange("(h p) -> p h", p=128), slow=True)
            t_sm = SP.dma(c_in[7], blcol, ap["gla_out_g_2"][0].rearrange("(h p) -> p h", p=128), slow=True)
            SP.dma(c_in[8], lng, wide(ap["gmlp_ln_g_2"][0], 512))
            t_ln = SP.dma(c_in[8], lnb, wide(ap["gmlp_ln_b_2"][0], 512))

            tk = {}

            def post_zlr(b, t):
                tk["zl"] = rest[b] = AC.op(lambda e: e.activation(zl[0:16, :], ps[b][0:16, :], ACT.Copy), t)

            def keep(dst, name, scale=1.0):
                def post(b, t):
                    tk[name] = rest[b] = AC.op(lambda e: e.activation(dst, ps[b][:], ACT.Copy, scale=scale), t)
                return post

            def gate():
                for half in range(2):
                    b = bank()

                    def issue(e, half=half, b=b):
                        e.matmul(ps[b][:], ones[0:1, :], gb[0:1, :], start=True, stop=True,
                                 skip_group_check=True)
                        for i in range(2):
                            t = half * 2 + i
                            m = e.matmul(ps[b][:, i * 256:i * 256 + 256], zl[0:16, t * 128:t * 128 + 128], gw[0:16, :],
                                         start=False, stop=True, skip_group_check=True)
                        return m
                    t = PE.op(issue, tk["zl"], t_sm, rest[b], t_ones)
                    low = la[:, 2 * half:2 * half + 2, :].rearrange("p t c -> p (t c)")
                    ln = ex[half]
                    a = AC.op(lambda e, b=b, ln=ln: e.activation(ln, ps[b][:], ACT.Abs), t)
                    m = DV.op(lambda e, b=b, low=low: e.tensor_scalar(low, ps[b][:], 0.0, None, ALU.min), a)
                    rest[b] = m
                    a = AC.op(lambda e, ln=ln: e.activation(ln, ln, ACT.Exp, scale=-1.0), a)
                    a = AC.op(lambda e, ln=ln: e.activation(ln, ln, ACT.Ln, bias=1.0), a)
                    tk["la", half] = DV.op(lambda e, ln=ln, low=low: e.tensor_tensor(low, low, ln, ALU.subtract), m, a)

            def cumulate(p):
                b = bank()

                def issue(e):
                    for t in range(4):
                        m = e.matmul(ps[b][:, t * 128:t * 128 + 128], la[:, t, p * 128:p * 128 + 128], tri[:],
                                     start=True, stop=True)
                    return m
                t = PE.op(issue, tk["la", 0], tk["la", 1], t_tri, rest[b])
                tk["cum", p] = rest[b] = DV.op(lambda e: e.tensor_copy(cum[p], ps[b][:]), t)

            def decays(p):
                c3 = cum[p].rearrange("p (n i) -> p n i", n=8)
                x0, x1 = ex
                a = AC.op(lambda e: e.activation(x0, cum[p], ACT.Exp), tk["cum", p], tk["la", 0], tk["la", 1], tk.get("ex0"))
                d = DV.op(lambda e: e.tensor_copy(dec[:, p * 8:p * 8 + 8],
                                                  x0.rearrange("p (n i) -> p n i", n=8)[:, :, 63]), a)
                q = DV.op(lambda e: e.tensor_tensor(qe[p], qe[p], x0, ALU.mult), a, tk["q", p])
                tk["dec", p], tk["qe", p] = d, q
                l = DV.op(lambda e: e.tensor_tensor(x1.rearrange("p (n i) -> p n i", n=8),
                                                    c3[:, :, 63:64].broadcast_to([128, 8, 64]), c3, ALU.subtract),
                          tk["cum", p], tk["la", 0], tk["la", 1], tk.get("ex1"))
                l = AC.op(lambda e: e.activation(x1, x1, ACT.Exp), l)
                l = DV.op(lambda e: e.tensor_tensor(x1, x1, ke[p], ALU.mult), l, tk["k", p])
                tk["kdT", p] = l
                a = AC.op(lambda e: e.activation(x0, cum[p], ACT.Exp, scale=-1.0), d, q)
                tk["ke", p] = tk["ex0"] = DV.op(lambda e: e.tensor_tensor(ke[p], ke[p], x0, ALU.mult), a, l)
                b = bank()

                def issue(e):
                    for t in range(4):
                        m = e.transpose(ps[b][:, t * 128:t * 128 + 128], x1[:, t * 128:t * 128 + 128], ident[:])
                    return m
                t = PE.op(issue, l, rest[b])
                tk["ex1"] = t
                tk["kd", p] = rest[b] = AC.op(lambda e: e.activation(
                    kd[p], ps[b][:].rearrange("p (t c) -> p t c", t=4), ACT.Copy), t)

            def updates(p):
                banks, made = [], []
                for odd in range(2):
                    rows = slice(64 * odd, 64 * odd + 64)
                    b = bank()

                    def issue(e, odd=odd, rows=rows, b=b):
                        for n in range(odd, 7, 2):
                            for a in range(2):
                                c = (n // 2) * 128
                                m = e.matmul(ps[b][64 * a:64 * a + 64, c:c + 128],
                                             kd[p][rows, n // 2, a * 64:a * 64 + 64],
                                             vb[rows, n // 2, (2 * p + a) * 128:(2 * p + a) * 128 + 128],
                                             start=True, stop=True)
                        return m
                    banks.append(b)
                    made.append(PE.op(issue, tk["kd", p], tk["vb"], rest[b]))
                for n in range(7):
                    c = (n // 2) * 128
                    u = ps[banks[n % 2]][:, c:c + 128]
                    s = p * 7 + n
                    if n == 0:
                        a = DV.op(lambda e, u=u, s=s: e.tensor_copy(St[:, s, :], u), made)
                    else:
                        a = DV.op(lambda e, u=u, s=s, n=n: e.scalar_tensor_tensor(
                            St[:, s, :], St[:, s - 1, :], dec[:, p * 8 + n:p * 8 + n + 1], u,
                            ALU.mult, ALU.add), a, tk["dec", p])
                    rest[banks[n % 2]] = a
                tk["S", p] = a

            def inner(h):
                p, a = divmod(h, 2)
                rows = slice(64 * a, 64 * a + 64)
                b = bank()

                def issue(e):
                    for t in range(4):
                        c = slice(t * 128, t * 128 + 128)
                        m = e.matmul(ps[b][:, c], ke[p][rows, c], qe[p][rows, c], start=True, stop=True)
                    return m
                t = PE.op(issue, tk["ke", p], tk["qe", p], rest[b])
                s_ = sc[h % 2]
                a_ = AC.op(lambda e: e.activation(s_, ps[b][:].rearrange("p (t c) -> p t c", t=4), ACT.Copy), t,
                           tk.get(("o", h - 2)))
                rest[b] = a_
                m = PL.op(lambda e: e.affine_select(out=s_, in_=s_, compare_op=ALU.is_ge, fill=0.0, base=0,
                                                    pattern=[[0, 4], [1, 128]], channel_multiplier=-1), a_, last_pool())
                tk["sc", h] = PL.op(lambda e: e.memset(s_[0:64, :, 64:128], 0.0), m, last_pool())

            def outer(h):
                p, a = divmod(h, 2)
                rows = slice(64 * a, 64 * a + 64)
                b = bank(hold=True)
                s_ = sc[h % 2]

                def issue(e):
                    for t in range(4):
                        m = e.matmul(ps[b][:, t * 128:t * 128 + 128], vb[:, t, h * 128:h * 128 + 128], s_[:, t, :],
                                     start=(t == 0), stop=(t == 3), skip_group_check=True)
                        for n in (2 * t, 2 * t + 1):
                            if n:
                                m = e.matmul(ps[b][:, n * 64:n * 64 + 64], St[rows, p * 7 + n - 1, :],
                                             qe[p][rows, n * 64:n * 64 + 64], start=False, stop=(n == 7),
                                             skip_group_check=True)
                    return m
                t = PE.op(issue, tk["sc", h], tk["vb"], tk["S", p], rest[b])
                tk["o", h] = t
                tk["sq"] = AC.op(lambda e: e.activation(sq, ps[b][:], ACT.Square), t, tk.get("sq_free"))
                tk["ob", h] = b

            def outer_norm(h):
                b = tk["ob", h]
                b2 = bank()
                m = PE.op(lambda e: e.matmul(ps[b2][:], ones[:], sq, start=True, stop=True), tk["sq"], rest[b2])
                a = AC.op(lambda e: e.activation(rinv, ps[b2][:], ACT.Ln, bias=eps6, scale=1.0 / 128), m, t_eps6,
                          tk.get("rinv_free"))
                rest[b2] = a
                a = AC.op(lambda e: e.activation(rinv, rinv, ACT.Exp, scale=-0.5), a)
                tk["sq_free"] = a
                tk["on", h] = DV.op(lambda e: e.scalar_tensor_tensor(
                    on[:, h, :], ps[b][:], blcol[:, h:h + 1], rinv, ALU.mult, ALU.mult), a, t_sm)
                tk["rinv_free"] = tk["on", h]
                let_go(b, tk["on", h])

            def post_zg(h):
                def post(b, t):
                    s = AC.op(lambda e: e.activation(ub, ps[b][:], ACT.Silu), t, tk.get("ub_free"))
                    rest[b] = s
                    o = DV.op(lambda e: e.tensor_tensor(of, ub, on[:, h, :], ALU.mult), s, tk["on", h],
                              tk.get("of_free"))
                    tk["ub_free"] = o
                    hi = AC.op(lambda e: e.activation(hh[:, 4 + h, :], of, ACT.Copy), o)
                    lo = DV.op(lambda e: e.tensor_tensor(hl[:, 4 + h, :], of, f32(hh[:, 4 + h, :]), ALU.subtract), hi)
                    tk["of_free"] = lo
                    h_ready[4 + h] = [hi, lo]
                return post

            def rows_half(name, dst, act, extra=None):
                banks = {}

                def piece(kb):
                    if kb == 0:
                        for t in range(4):
                            banks[t] = bank(hold=True)
                    j, wh, wl, ready = W.take()
                    for t in range(4):
                        def issue(e, t=t):
                            for k in (0, 1):
                                a = slice(t * 128, t * 128 + 128)
                                m = mm3(e, ps[banks[t]][:], xh[:, 2 * kb + k, a], xl[:, 2 * kb + k, a],
                                        wh[:, k, :], wl[:, k, :], kb + k == 0, 2 * kb + k == 7)
                            return m
                        need = [ready, rest[banks[t]] if kb == 0 else None, x_ready]
                        if kb == 3 or t == 3:
                            tok = PE.op(issue, need)
                        else:
                            PE.quiet(issue, need)
                        if t == 3:
                            W.done(j, tok)
                        if kb == 3:
                            b = banks[t]
                            s = AC.op(lambda e, b=b, t=t: e.activation(dst[:, t, :], ps[b][:], act), tok)
                            let_go(b, s)
                            if extra:
                                s = extra(t, s)
                            tk.setdefault(name, []).append(s)
                return [lambda kb=kb: piece(kb) for kb in range(4)]

            def v_norm(t, ready):
                m = moments(t, 0, v[:, t, :], ready)
                r = inv_std(t, 1, eps6, t_eps6, True, m)
                a = DV.op(lambda e: e.scalar_tensor_tensor(v[:, t, :], v[:, t, :], mv[:, 2 * t:2 * t + 1], lng,
                                                           ALU.subtract, ALU.mult), r, t_ln)
                return DV.op(lambda e: e.scalar_tensor_tensor(v[:, t, :], v[:, t, :], rs[:, t:t + 1], lnb,
                                                              ALU.mult, ALU.add), a)

            def turn_ws():
                b = bank()

                def issue(e):
                    for h in range(4):
                        m = e.transpose(ps[b][:, h * 128:h * 128 + 128], wsb[:, h, :], ident[:])
                    return m
                t = PE.op(issue, t_ws, rest[b])
                a = rest[b] = AC.op(lambda e: e.activation(wT, ps[b][:].rearrange("p (t c) -> p t c", t=4), ACT.Copy), t)
                tk["wT"] = PL.op(lambda e: e.memset(wT[64:128, :, 0:64], 0.0), a, last_pool())

            def mixed(h):
                b = bank()

                def issue(e):
                    e.matmul(ps[b][:].rearrange("p (n i) -> p n i", n=4), ones[0:1, :],
                             bsr[0:1, h * 128:h * 128 + 128].unsqueeze(1).broadcast_to([1, 4, 128]),
                             start=True, stop=True, skip_group_check=True)
                    for t in range(4):
                        m = e.matmul(ps[b][:, t * 128:t * 128 + 128], v[:, t, h * 128:h * 128 + 128], wT[:, h, :],
                                     start=False, stop=True, skip_group_check=True)
                    return m
                tk["mx", h] = (b, PE.op(issue, tk["v"], tk["wT"], t_sm, rest[b]))

            def post_zu(h):
                def post(b, t):
                    s = AC.op(lambda e: e.activation(ub, ps[b][:], ACT.Gelu_apprx_tanh), t, tk.get("ub_free"))
                    rest[b] = s
                    mixed(h)
                    mb, mt = tk["mx", h]
                    o = DV.op(lambda e: e.tensor_tensor(outa[:, h, :], ps[mb][:], ub, ALU.mult), s, mt,
                              tk["o", 3], tk.get("ub_free"))
                    rest[mb] = o
                    tk["ub_free"] = o
                    q = AC.op(lambda e: e.activation([sq, of][h % 2], outa[:, h, :], ACT.Square), o,
                              tk.get(("sqm", h - 2)), tk.get("of_free"), tk.get("sq_free"))
                    if h == 0:
                        tk["rb"] = bank(hold=True)
                    rb = tk["rb"]
                    tk["sqm", h] = PE.op(lambda e: e.matmul(ps[rb][:], ones[:], [sq, of][h % 2], start=(h == 0),
                                                            stop=(h == 3)), q, rest[rb] if h == 0 else None)
                return post

            for f in project(post_zlr):
                f()
            pk = [project(keep(ke[p], ("k", p))) for p in range(2)]
            pq = [project(keep(qe[p], ("q", p), 0.125)) for p in range(2)]
            for f in pk[0]:
                f()
            gate()
            turn_ws()
            for f in pk[1]:
                f()
            for f in pq[0]:
                f()
            cumulate(0)
            cumulate(1)
            for f in pq[1]:
                f()
            for f in rows_half("vb", vb, ACT.Copy):
                f()
            decays(0)
            pv = rows_half("v", v, ACT.Gelu_apprx_tanh, v_norm)
            for f in pv[0:2]:
                f()
            decays(1)
            inner(0)
            inner(1)
            updates(0)
            for f in pv[2:4]:
                f()
            updates(1)
            outer(0)
            fill = []
            for h in range(4):
                fill += project(post_zg(h))
            outer_norm(0)
            order = [lambda: inner(2), lambda: outer(1), lambda: outer_norm(1), lambda: inner(3),
                     lambda: outer(2), lambda: outer_norm(2), lambda: outer(3), lambda: outer_norm(3)]
            at = [1, 1, 2, 5, 5, 6, 9, 10]
            for i, f in enumerate(fill):
                for n, o in zip(at, order):
                    if n == i:
                        o()
                f()
            for h in range(4):
                for f in project(post_zu(h)):
                    f()
            rb = tk["rb"]
            a = AC.op(lambda e: e.activation(rinv, ps[rb][:], ACT.Ln, bias=eps6, scale=1.0 / 512), tk["sqm", 3],
                      tk["rinv_free"])
            let_go(rb, a)
            a = AC.op(lambda e: e.activation(rinv, rinv, ACT.Exp, scale=-0.5), a)
            for h in range(4):
                o = DV.op(lambda e, h=h: e.scalar_tensor_tensor(outa[:, h, :], outa[:, h, :], gocol[:, h:h + 1], rinv,
                                                                ALU.mult, ALU.mult), a)
                hi = AC.op(lambda e, h=h: e.activation(hh[:, h, :], outa[:, h, :], ACT.Copy), o)
                lo = DV.op(lambda e, h=h: e.tensor_tensor(hl[:, h, :], outa[:, h, :], f32(hh[:, h, :]), ALU.subtract), hi)
                h_ready[h] = [hi, lo]

        mixer()
        if upto == 6:
            o = [DV.op(lambda e, k=k: e.tensor_tensor(x[:, k // 2, (k % 2) * 512:(k % 2) * 512 + 512],
                                                     f32(hh[:, k, :]), f32(hl[:, k, :]), ALU.add), h_ready[k])
                 for k in range(8)]
            return finish(nc, locals(), o)

        mb = ar(3072, 4096).rearrange("p (t c) -> p t c", t=4)
        all_h = [h_ready[k] for k in range(8)]
        tg = load_g(0, ap["post_mix_g_2"][0], all_h)
        tp = load_g(2, ap["pre_ff_g_2"][0], all_h)
        fresh = []

        def add_rms(t, m, tg):
            r = inv_std(t, 2, eps6, t_eps6, False, m)
            a = DV.op(lambda e: e.scalar_tensor_tensor(mb[:, t, :], mb[:, t, :], rs[:, t:t + 1], gvec[0],
                                                       ALU.mult, ALU.mult), r, tg)
            last_g[0] = a
            return DV.op(lambda e: e.tensor_tensor(x[:, t, :], x[:, t, :], mb[:, t, :], ALU.add), a)

        def post_w(nh, t, b, token):
            cols = slice(nh * 512, nh * 512 + 512)
            a = rest[b] = AC.op(lambda e: e.activation(mb[:, t, cols], ps[b][:], ACT.Copy), token)
            m = moments(t, nh, mb[:, t, cols], a)
            if nh == 0:
                return None
            return rms_features(t, tp, fresh, add_rms(t, m, tg))

        run_all(tokens_out(post_w, hh, hl, lambda k, t: h_ready[k], 8))
        x_ready[:] = fresh
        if upto == 7:
            return finish(nc, locals(), x_ready)

        rbuf = [ar(7168 + i * 512, 512) for i in range(2)]
        fbuf = [ar(8192 + i * 512, 512) for i in range(2)]
        free, n = {}, [0]
        tg = load_g(0, ap["post_ff_g_2"][0], last_g[0])
        c_out = count("s_out")
        prev = None
        for g in range(4):
            for f in range(8):
                def post(b, t, f=f):
                    i = n[0] % 2
                    s = AC.op(lambda e: e.activation(rbuf[i], ps[b][:], ACT.Relu), t, free.get(n[0] - 2))
                    o = DV.op(lambda e: e.tensor_tensor(fbuf[i], rbuf[i], ps[b][:], ALU.mult), s)
                    rest[b] = o
                    hi = AC.op(lambda e: e.activation(hh[:, f, :], fbuf[i], ACT.Copy), o, prev)
                    lo = DV.op(lambda e: e.tensor_tensor(hl[:, f, :], fbuf[i], f32(hh[:, f, :]), ALU.subtract), hi, prev)
                    h_ready[f] = [hi, lo]
                    free[n[0]] = lo
                    n[0] += 1
                for piece in project(post):
                    piece()

            def post_f(nh, t, b, token, g=g):
                cols = slice(nh * 512, nh * 512 + 512)
                if g == 0:
                    a = AC.op(lambda e: e.activation(mb[:, t, cols], ps[b][:], ACT.Copy), token)
                else:
                    a = DV.op(lambda e: e.tensor_tensor(mb[:, t, cols], mb[:, t, cols], ps[b][:], ALU.add), token)
                rest[b] = a
                if g < 3:
                    return None
                m = moments(t, nh, mb[:, t, cols], a)
                if nh == 0:
                    return None
                a = add_rms(t, m, tg)
                SP.dma(c_out, out[0, t * 128:(t + 1) * 128, :], x[:, t, :], a)
                return None
            run_all(tokens_out(post_f, hh, hl, lambda k, t: h_ready[k], 8))
            prev = W.done_t[W.taken - 1]
        SP.wait((c_out, c_out.value))
        emit(nc, ctx, PE, AC, DV, PL, SP)


def emit(nc, ctx, PE, AC, DV, PL, SP):
    block = ctx.enter_context(nc.Block())
    block.tensor(PE.play)
    block.scalar(AC.play)
    block.vector(DV.play)
    block.gpsimd(PL.play)
    block.sync(SP.play)


def finish(nc, l, tokens):
    SP, x, out = l["SP"], l["x"], l["out"]
    c = l["count"]("s_fin")
    SP.wait((l.get("t_toep") or [None])[-1], tokens, (l["DV"].count, l["DV"].count.value))
    for t in range(4):
        SP.dma(c, out[0, t * 128:(t + 1) * 128, :], x[:, t, :])
    SP.wait((c, c.value))
    emit(nc, l["ctx"], l["PE"], l["AC"], l["DV"], l["PL"], SP)


def constants():
    inv = (np.float32(10000.0) ** (-np.arange(0, 64, 2, dtype=np.float32) / np.float32(64))).astype(np.float32)
    ang = np.arange(S, dtype=np.float32)[:, None] * inv[None, :]
    cos, sin = np.cos(ang.astype(np.float64)), np.sin(ang.astype(np.float64))
    d = np.arange(128) % 32
    c = cos.T[d].astype(np.float32)
    s = (sin.T[d] * np.where(np.arange(128) < 64, 1.0, -1.0)[:, None]).astype(np.float32)
    m = ((np.arange(128) // 32) % 2).astype(np.float32)
    j, i = np.arange(128)[:, None], np.arange(128)[None, :]
    tri = np.where((j <= i) & (j // 64 == i // 64), np.float32(1 / 16), np.float32(0)).astype(np.float32)
    return {
        "c_ident": np.eye(128, dtype=np.float32), "c_cos": np.ascontiguousarray(c),
        "c_sin": np.ascontiguousarray(s), "c_mask": np.ascontiguousarray(np.stack([1 - m, m], 1)), "c_tri": tri,
    }


def halves_first(w):
    qk = w[..., :2 * D].reshape(D, 16, 2, 2, 32).transpose(0, 1, 3, 2, 4).reshape(1, D, 2 * D)
    return np.concatenate([qk, w[..., 2 * D:]], axis=-1)


_INS = ["x", "a_w_qkv", "a_lambda", "a_subln_g", "a_w_o", "kv_w", "b_w_q", "b_rel_bias", "b_w_o", "ln_g", "ln_b",
        "ffn_w_in", "ffn_w_out", "pre_mix_g_2", "w_in_2", "gmlp_ln_g_2", "gmlp_ln_b_2", "gmlp_ws_2", "gmlp_bs_2",
        "gmlp_out_g_2", "gla_gate_w_2", "gla_gate_b_2", "gla_out_g_2", "w_out_2", "post_mix_g_2", "pre_ff_g_2",
        "w_ff1_2", "w_ff2_2", "post_ff_g_2"]


def kernel(**inputs):
    import concourse.bacc as _bacc
    from concourse.bass_utils import run_bass_kernel_spmd as _run

    nc = _bacc.Bacc("TRN2", target_bir_lowering=False, num_devices=1)
    arrays, aps = {}, {}
    given = {name: np.ascontiguousarray(inputs[name]) for name in _INS}
    given["a_w_qkv"] = halves_first(given["a_w_qkv"])
    given.update(constants())
    for name, a in given.items():
        arrays[f"in_{name}"] = a
        aps[name] = nc.dram_tensor(f"in_{name}", a.shape, mybir.dt.from_np(a.dtype), kind="ExternalInput").ap()
    out = nc.dram_tensor("out_0", (1, S, D), F32, kind="ExternalOutput").ap()
    build(nc, aps, out)
    r = _run(nc, [arrays], core_ids=[0])
    return r.results[0]["out_0"]
```

```python
import math
from contextlib import ExitStack

import numpy as np

import concourse.bass as bass
from concourse import mybir

F32 = mybir.dt.float32
F32R = mybir.dt.float32r
ALU = mybir.AluOpType
ACT = mybir.ActivationFunctionType
AX = mybir.AxisListType.X

D = 1024
S = 512
FF = 2816
FF2 = 4096
NEG = float(np.finfo(np.float32).min)
ALPHA = 4 ** 0.25
LAMBDA_INIT = 0.8 - 0.6 * math.exp(0.0)
ELEN = 640


class Count:

    def __init__(self, sem):
        self.sem, self.value = sem, 0

    def add(self, n):
        self.value += n
        return (self, self.value)


def flat(waits):
    for w in waits:
        if w is None:
            continue
        if isinstance(w, list):
            yield from flat(w)
        else:
            yield w


class Queue:

    def __init__(self, count):
        self.count, self.items, self.waited = count, [], {}

    def wait(self, *tokens):
        for count, value in flat(tokens):
            if self.waited.get(count, 0) < value:
                self.waited[count] = value
                self.items.append(lambda e, c=count, v=value: e.wait_ge(c.sem, v))

    def op(self, issue, *tokens):
        self.wait(*tokens)
        self.items.append(lambda e: issue(e).then_inc(self.count.sem, 1))
        return self.count.add(1)

    def quiet(self, issue, *tokens):
        self.wait(*tokens)
        self.items.append(issue)

    def dma(self, count, out, in_, *tokens, slow=False):
        self.wait(*tokens)
        self.items.append(lambda e: e.dma_start(out, in_, allow_slow_non_contiguous=slow).then_inc(count.sem, 16))
        return count.add(16)

    def play(self, engine):
        for item in self.items:
            item(engine)


def f32(ap):
    return ap.bitcast(F32)


def run_all(items):
    for item in items:
        item()


def build(nc, ap, out):
    with ExitStack() as ctx:
        def sb(name, shape, dt=F32):
            return ctx.enter_context(nc.sbuf_tensor(name, shape, dt))

        def count(name):
            return Count(ctx.enter_context(nc.semaphore(name)))

        PE, AC, DV, PL, SP = (Queue(count("s_" + n)) for n in ("pe", "act", "dve", "pool", "sp"))

        ps = [ctx.enter_context(nc.psum_tensor(f"ps{i}", [128, 512], F32)) for i in range(8)]
        RING = 4
        raw = sb("raw", [128, RING, 1024])
        whi = sb("whi", [128, RING, 1024], F32R)
        wlo = sb("wlo", [128, RING, 1024], F32R)
        x = sb("x", [128, 4, D])
        xh = sb("xh", [128, 8, S], F32R)
        xl = sb("xl", [128, 8, S], F32R)
        hh = sb("hh", [128, 8, S], F32R)
        hl = sb("hl", [128, 8, S], F32R)
        arena = sb("arena", [128, 19200])
        ident = sb("ident", [128, 128])
        ones = sb("ones", [128, 128])
        stat = sb("stat", [128, 512])
        small = sb("small", [128, 128])

        def ar(start, n):
            return arena[:, start:start + n]

        rest = [None] * 8
        turn = [0]
        held = set()

        def bank(hold=False):
            while turn[0] % 8 in held:
                turn[0] += 1
            b = turn[0] % 8
            turn[0] += 1
            if hold:
                held.add(b)
            return b

        def let_go(b, token):
            held.discard(b)
            rest[b] = token

        eps5, eps6 = small[:, 0:1], small[:, 1:2]
        nlam, g8 = small[:, 2:3], small[:, 3:4]
        mask0, mask1 = small[:, 4:5], small[:, 5:6]
        gocol, blcol = small[:, 6:10], small[:, 10:14]
        dec = small[:, 16:32]
        bst = small[:, 32:80]
        mv = small[:, 80:88]
        rs = small[:, 88:96]
        lsum = small[:, 96:104]

        c_in = [count(f"s_in{i}") for i in range(12)]
        c_x = [count(f"s_x{i}") for i in range(4)]
        t_ident = SP.dma(c_in[0], ident[:], ap["c_ident"])
        for t in range(4):
            SP.dma(c_x[t], x[:, t, :], ap["x"][0, t * 128:(t + 1) * 128, :])
        x_in = [(c_x[t], 16) for t in range(4)]

        def last_pool():
            return (PL.count, PL.count.value)

        t_ones = PL.op(lambda e: e.memset(ones[:], 1.0))
        t_eps5 = PL.op(lambda e: e.memset(eps5, 1e-5), last_pool())
        t_eps6 = PL.op(lambda e: e.memset(eps6, 1e-6), last_pool())

        plan = []

        def plan_cols(w, c0, n=8, k0=0):
            plan.append((w[k0 * 128:(k0 + n) * 128, c0:c0 + 128], n, 128))

        def plan_rows(w, k0, c0):
            plan.append((w[k0 * 128:(k0 + 2) * 128, c0:c0 + 512], 2, 512))

        def plan_out(w, k0, nk, k_first=0, times=1):
            for nh in list(range(2)) * times:
                for k in range(0, nk, 2):
                    plan_rows(w, k0 + (k_first + k) % nk, nh * 512)

        qkv, kvw, bq = ap["a_w_qkv"][0], ap["kv_w"], ap["b_w_q"][0]
        win2 = ap["w_in_2"][0]
        groups = [(0, 8), (8, 8), (16, 6)]
        for nh in range(2):
            for k in range(0, 8, 2):
                plan_rows(qkv, k, 2048 + nh * 512)
        for h in range(8):
            plan_cols(qkv, h * 128)
            plan_cols(qkv, 1024 + h * 128)
        plan_out(ap["a_w_o"][0], 0, 8)

        def plan_ffn(layer, times=1):
            for f0, nf in groups:
                for f in range(f0, f0 + nf):
                    plan_cols(ap["ffn_w_in"][layer], f * 128)
                    plan_cols(ap["ffn_w_in"][layer], FF + f * 128)
                plan_out(ap["ffn_w_out"][layer], f0, nf, times=times if f0 == 16 else 1)

        plan_ffn(0, times=2)
        for nh in range(2):
            for k in range(0, 8, 2):
                plan_rows(kvw, k, 1024 + nh * 512)
        for p in range(8):
            plan_cols(bq, p * 128)
            plan_cols(kvw, p * 128)
        plan_out(ap["b_w_o"][0], 0, 8)
        plan_ffn(1, times=2)
        zlr_at = len(plan)
        plan_cols(win2, 2448)
        for c in (1280, 1408, 1024, 1152):
            plan_cols(win2, c)
        for c in (1536, 512):
            for k in range(0, 8, 2):
                plan_rows(win2, k, c)
        for c in range(4):
            plan_cols(win2, 2048 + c * 128)
        for c in range(4):
            plan_cols(win2, c * 128)
        plan_out(ap["w_out_2"][0], 0, 8, 4, times=2)
        for g in range(4):
            for f in range(8):
                plan_cols(ap["w_ff1_2"][0], (g * 8 + f) * 128)
            plan_out(ap["w_ff2_2"][0], g * 8, 8)

        class Weights:
            def __init__(self):
                self.c = [count(f"s_w{i}") for i in range(RING)]
                self.loaded, self.split_n, self.taken = 0, 0, 0
                self.by_pool = False
                self.dma_t, self.hi_t, self.lo_t, self.done_t = {}, {}, {}, {}
                while self.loaded < RING:
                    self.load()

            def load(self):
                j = self.loaded
                if j >= len(plan):
                    return
                src, n, cols = plan[j]
                s = j % RING
                dst = raw[:, s, :].rearrange("p (k c) -> p k c", k=n)
                free = [self.hi_t.get(j - RING), self.lo_t.get(j - RING)]
                if j == zlr_at:
                    view = win2.rearrange("(k p) c -> p k c", p=128)
                    SP.dma(self.c[s], dst[:, :, 0:16], view[:, :, 2560:2576], free)
                    t = SP.dma(self.c[s], dst[:, :, 16:128], view[:, :, 2448:2560])
                else:
                    t = SP.dma(self.c[s], dst, src.rearrange("(k p) c -> p k c", p=128), free)
                self.dma_t[j] = t
                self.loaded += 1

            def pump(self):
                while self.split_n < min(len(plan), self.taken + RING - 1):
                    j = self.split_n
                    if j >= RING and j - RING not in self.done_t:
                        return
                    s = j % RING
                    free = self.done_t.get(j - RING)
                    self.hi_t[j] = AC.op(lambda e, s=s: e.activation(whi[:, s, :], raw[:, s, :], ACT.Copy),
                                         self.dma_t[j], free)
                    q = PL if self.by_pool else DV
                    self.lo_t[j] = q.op(lambda e, s=s: e.tensor_tensor(wlo[:, s, :], raw[:, s, :],
                                                                       f32(whi[:, s, :]), ALU.subtract),
                                        self.dma_t[j], self.hi_t[j], free, last_pool() if self.by_pool else None)
                    self.split_n += 1
                    self.load()

            def take(self):
                j = self.taken
                self.taken += 1
                self.pump()
                assert j < self.split_n
                _, n, cols = plan[j]
                s = j % RING
                h = whi[:, s, :].rearrange("p (k c) -> p k c", k=n)
                low = wlo[:, s, :].rearrange("p (k c) -> p k c", k=n)
                return j, h, low, [self.hi_t[j], self.lo_t[j]]

            def done(self, j, token):
                self.done_t[j] = token
                self.pump()

        def table(name):
            AC.quiet(lambda e: e.preload_act_table_set(name))

        W = Weights()
        table("natural_log_exp_and_others")

        def mm3(e, o, ah, al, bh, bl, start, stop):
            e.matmul(o, ah, bh, start=start, stop=False)
            e.matmul(o, ah, bl, start=False, stop=False)
            return e.matmul(o, al, bh, start=False, stop=stop)

        x_tile = [None] * 4
        carry = []
        h_ready = [None] * 8

        waiting = []

        def settle():
            while waiting:
                waiting.pop(0)()

        def project(post):
            st = {}

            def piece(i):
                if i == 0:
                    st["w"] = W.take()
                    st["b"] = bank(hold=True)
                j, wh, wl, ready = st["w"]
                b = st["b"]

                def issue(e):
                    for k in (2 * i, 2 * i + 1):
                        m = mm3(e, ps[b][:], wh[:, k, :], wl[:, k, :], xh[:, k, :], xl[:, k, :], k == 0, k == 7)
                    return m

                if i < 3:
                    PE.quiet(issue, *([ready, rest[b], x_tile] if i == 0 else []))
                else:
                    t = PE.op(issue)
                    W.done(j, t)
                    held.discard(b)
                    post(b, t)

            return [lambda i=i: piece(i) for i in range(4)]

        def project_first(posts, middle):
            jobs = [(W.take(), bank(hold=True), post) for post in posts]
            settle()
            for part in range(2):
                c = slice(part * 256, part * 256 + 256)
                for (j, wh, wl, ready), b, post in jobs:
                    def issue(e, wh=wh, wl=wl, b=b, c=c):
                        for k in range(8):
                            m = mm3(e, ps[b][:, c], wh[:, k, :], wl[:, k, :], xh[:, k, c], xl[:, k, c], k == 0, k == 7)
                        return m
                    need = [ready, rest[b]] + x_tile[2 * part:2 * part + 2]
                    if part:
                        t = PE.op(issue, need)
                        W.done(j, t)
                        held.discard(b)
                        post(b, t)
                    else:
                        PE.quiet(issue, need)
                if not part:
                    run_all(middle)
                    W.by_pool = False

        def projections(posts, functions):
            def first():
                middle, carry[:] = list(carry), []
                project_first(posts[:3], middle + [lambda: table(functions)])
            return [first] + [piece for post in posts[3:] for piece in project(post)]

        def tokens_out(post, ah, al, ready_of, nk, k_first=0, ends=False, pairs=False):
            later, st, pieces = [], {}, []

            def busy():
                W.by_pool = True
                table("sqrt_and_others")

            def piece(nh, tiles, k0, t):
                first, last = k0 == k_first, k0 == (k_first - 2) % nk
                if first and t == tiles[0]:
                    for tile in tiles:
                        st["b", tile] = bank(hold=True)
                if t == tiles[0]:
                    st[k0] = W.take()
                    if k0 == k_first:
                        settle()
                j, wh, wl, ready = st[k0]
                b = st["b", t]

                def issue(e):
                    for k in (0, 1):
                        a = slice(t * 128, t * 128 + 128)
                        m = mm3(e, ps[b][:], ah[:, k0 + k, a], al[:, k0 + k, a],
                                wh[:, k, :], wl[:, k, :], first and k == 0, last and k == 1)
                    return m
                need = [ready, rest[b] if first else None, ready_of(k0, t), ready_of(k0 + 1, t)]
                if t < tiles[-1] and not last:
                    PE.quiet(issue, need)
                    return
                token = PE.op(issue, need)
                if t == tiles[-1]:
                    W.done(j, token)
                if last:
                    held.discard(b)
                    settle()
                    if later and not pairs:
                        later.pop(0)()
                    more = post(nh, t, b, token)
                    if more:
                        later.append(more)

            stages = [(nh, tiles) for tiles in ((0, 1), (2, 3)) for nh in range(2)] if pairs else [
                (nh, (0, 1, 2, 3)) for nh in range(2)]
            for nh, tiles in stages:
                blocks = [(k_first + k) % nk for k in range(0, nk, 2)]
                n_tiled = min(3, len(blocks))
                if nh == 0 and ah is hh:
                    runs = [[k] for k in blocks]
                elif nh == 0:
                    runs = [blocks[:n_tiled]] + [[k] for k in blocks[n_tiled:]]
                else:
                    runs = [[k] for k in blocks[:-n_tiled]] + [blocks[-n_tiled:]]
                for run in runs:
                    if ends and nh == 1 and tiles[0] == 0 and run is runs[-1]:
                        pieces.append(busy)
                    for t in tiles:
                        for k0 in run:
                            pieces.append(lambda nh=nh, tiles=tiles, k0=k0, t=t: piece(nh, tiles, k0, t))
                    if pairs and nh == 0 and tiles[0] == 2 and run in runs[-2:]:
                        pieces.append(lambda: later.pop(0)())

            def carry_on():
                carry.extend(later)
            pieces.append(carry_on)
            return pieces

        def to_features(t, src, ready):
            tokens = []
            for half in range(2):
                b = bank()

                def issue(e, half=half, b=b):
                    for k in range(4):
                        m = e.transpose(ps[b][:, k * 128:(k + 1) * 128],
                                        src[:, (half * 4 + k) * 128:(half * 4 + k + 1) * 128], ident[:])
                    return m
                tr = PE.op(issue, ready[half], rest[b], t_ident)
                dst = (slice(None), slice(half * 4, half * 4 + 4), slice(t * 128, t * 128 + 128))
                view = ps[b][:].rearrange("p (k c) -> p k c", k=4)
                hi = AC.op(lambda e, dst=dst, view=view: e.activation(xh[dst], view, ACT.Copy), tr)
                lo = DV.op(lambda e, dst=dst, view=view: e.tensor_tensor(xl[dst], view, f32(xh[dst]), ALU.subtract), hi)
                rest[b] = lo
                tokens += [hi, lo]
            x_tile[t] = tokens
            return None

        def moments(t, part, src, ready):
            return DV.op(lambda e: e.bn_stats(bst[:, t * 12 + part * 6:t * 12 + part * 6 + 6], src), ready)

        def inv_std(t, parts, eps, t_eps, plain, ready):
            m, r = mv[:, 2 * t:2 * t + 2], rs[:, t:t + 1]
            a = DV.op(lambda e: e.bn_aggr(m, bst[:, t * 12:t * 12 + 6 * parts]), ready)
            if not plain:
                a = DV.op(lambda e: e.scalar_tensor_tensor(m[:, 1:2], m[:, 0:1], m[:, 0:1], m[:, 1:2],
                                                           ALU.mult, ALU.add), a)
            s = AC.op(lambda e: e.activation(lsum[:, t:t + 1], m[:, 1:2], ACT.Sqrt, bias=eps), a, t_eps)
            return DV.op(lambda e: e.reciprocal(r, lsum[:, t:t + 1]), s)

        gvec = [ar(i * 1024, 1024) for i in range(3)]
        c_g = [count(f"s_g{i}") for i in range(3)]

        def load_g(i, v, *free):
            src = bass.AP(tensor=v.tensor, offset=v.offset, ap=[[0, 128], [1, 1024]])
            return SP.dma(c_g[i], gvec[i], src, *free)

        last_g = [None, None, None]

        def layer_norm(t, ready, tg, tb):
            r = inv_std(t, 2, eps5, t_eps5, True, ready)
            done = []
            for half in range(2):
                c = slice(half * 512, half * 512 + 512)
                a = DV.op(lambda e, c=c: e.scalar_tensor_tensor(x[:, t, c], x[:, t, c], mv[:, 2 * t:2 * t + 1],
                                                                gvec[0][:, c], ALU.subtract, ALU.mult), r, tg)
                done.append(DV.op(lambda e, c=c: e.scalar_tensor_tensor(x[:, t, c], x[:, t, c], rs[:, t:t + 1],
                                                                        gvec[1][:, c], ALU.mult, ALU.add), a, tb))
            return done

        def residual_norm(last_group=True, first_group=True, after=None):
            def post(nh, t, b, token):
                cols = slice(nh * 512, nh * 512 + 512)
                scale = ALPHA if first_group else 1.0
                a = DV.op(lambda e: e.scalar_tensor_tensor(x[:, t, cols], x[:, t, cols], scale, ps[b][:],
                                                           ALU.mult, ALU.add), token)
                rest[b] = a
                if not last_group:
                    return None
                m = moments(t, nh, x[:, t, cols], a)
                if nh == 0:
                    return None
                return after(t, m)
            return post

        def norm_then_features(row):
            l, r = divmod(row, 2)
            tg = load_g(0, ap["ln_g"][l, r], last_g[0])
            tb = load_g(1, ap["ln_b"][l, r], last_g[1])
            def after(t, m):
                a = layer_norm(t, m, tg, tb)
                last_g[0] = last_g[1] = a

                def pe():
                    to_features(t, x[:, t, :], a)
                return pe
            return after

        for t in range(4):
            to_features(t, x[:, t, :], [x_in[t], x_in[t]])

        BASE = 3072

        def not_busy():
            W.by_pool = False
            table("natural_log_exp_and_others")

        def values_out(V):
            tokens = []

            def post(nh, t, b, token):
                a = AC.op(lambda e: e.activation(V[:, t, nh * 512:nh * 512 + 512], ps[b][:], ACT.Copy), token)
                rest[b] = a
                tokens.append(a)
                return None
            pieces = tokens_out(post, xh, xl, lambda k, t: x_tile[t], 8)
            if carry:
                first, last = carry
                carry[:] = []
                pieces[9:9] = [last, not_busy]
                pieces[6:6] = [first]
            return tokens, pieces

        esb = ar(BASE + 15360, 640)
        e2 = nc.dram_tensor("bias_rows", [16, ELEN], F32, kind="Internal").ap()
        toep = nc.dram_tensor("bias_skewed", [16, 128 * ELEN], F32, kind="Internal").ap()
        c_b = [count(f"s_b{i}") for i in range(5)]
        rel = ap["b_rel_bias"][0]
        t_toep = []

        def bias_rows():
            t1 = SP.dma(c_b[0], esb[0:16, 256:640], rel[:, 1:385])
            t2 = SP.dma(c_b[0], esb[0:16, 0:2], rel[:, 0:2])
            t3 = PL.op(lambda e: e.tensor_copy(esb[0:16, 1:256], esb[0:16, 0:1].broadcast_to([16, 255])), t1, t2,
                       last_pool())
            return SP.dma(c_b[1], e2, esb[0:16, :], t3)

        def bias_skewed(h, n, ready):
            src = bass.AP(tensor=e2.tensor, offset=h * ELEN, ap=[[ELEN, n], [0, 128], [1, ELEN]])
            dst = bass.AP(tensor=toep.tensor, offset=h * 128 * ELEN, ap=[[128 * ELEN, n], [ELEN, 128], [1, ELEN]])
            t_toep.append(SP.dma(c_b[2], dst, src, ready))

        AHEAD_A = 8
        ORDER_A = "- t3 - S0 S1 F0 w F1 - T0 S2 T1 S3 F2 - - - F3 n T2 -".split()

        def attention_a(then):
            cosb, sinb = ar(BASE, 512), ar(BASE + 512, 512)
            qk = [[ar(BASE + 1024 + (n * 3 + i) * 512, 512) for i in range(3)] for n in range(2)]
            qk.append([ar(BASE + 13824 + i * 512, 512) for i in range(3)])
            V = ar(BASE + 4096, 4096).rearrange("p (t c) -> p t c", t=4)
            ebuf = [[ar(BASE + 8192 + (n * 2 + m) * 512, 512) for m in range(2)] for n in range(2)]
            aT = ar(BASE + 10240, 2048).rearrange("p (j q) -> p j q", j=4)
            tmp, sq, of = (ar(BASE + 12288 + i * 512, 512) for i in range(3))
            lam4 = ar(BASE + 12288, 256)
            t_cos = SP.dma(c_in[1], cosb, ap["c_cos"])
            t_sin = SP.dma(c_in[1], sinb, ap["c_sin"])
            t_mask = SP.dma(c_in[2], small[:, 4:6], ap["c_mask"])
            t_sub = SP.dma(c_in[3], g8, ap["a_subln_g"][0].rearrange("(p a) -> p a", a=1), slow=True)
            lp = ap["a_lambda"][0]
            t_lam = SP.dma(c_in[4], lam4, bass.AP(tensor=lp.tensor, offset=lp.offset, ap=[[0, 128], [1, 256]]))
            v_ready, pieces = values_out(V)
            run_all(pieces)
            t_g8 = DV.op(lambda e: e.tensor_scalar(g8, g8, 1.0 - LAMBDA_INIT, None, ALU.mult), t_sub)
            l1 = DV.op(lambda e: e.tensor_tensor_reduce(sq[:, 0:64], lam4[:, 0:64], lam4[:, 64:128], 1.0, 0.0,
                                                        ALU.mult, ALU.add, lsum[:, 0:1]), t_lam)
            l2 = DV.op(lambda e: e.tensor_tensor_reduce(sq[:, 64:128], lam4[:, 128:192], lam4[:, 192:256], 1.0, 0.0,
                                                        ALU.mult, ALU.add, lsum[:, 1:2]), t_lam)
            le = AC.op(lambda e: e.activation(lsum[:, 2:4], lsum[:, 0:2], ACT.Exp), l1, l2)
            l3 = DV.op(lambda e: e.tensor_tensor(nlam, lsum[:, 3:4], lsum[:, 2:3], ALU.subtract), le)
            t_nlam = DV.op(lambda e: e.tensor_scalar(nlam, nlam, -LAMBDA_INIT, None, ALU.add), l3)

            t_rows = bias_rows()
            qk_ready = {}
            qk_free = {}

            tmp_free = [None]

            def rope(h, which):
                def post(b, t):
                    q0, q1, k = qk[h % 3]
                    dst = k if which else q0
                    u0 = DV.op(lambda e: e.tensor_tensor(tmp[0:64, :], ps[b][64:128, :], sinb[64:128, :], ALU.mult),
                               t, t_sin, t_nlam, tmp_free[0])
                    u1 = DV.op(lambda e: e.tensor_tensor(tmp[64:128, :], ps[b][0:64, :], sinb[0:64, :], ALU.mult))
                    a = rest[b] = DV.op(lambda e: e.tensor_tensor(dst, ps[b][:], cosb, ALU.mult), t_cos,
                                        qk_free.get(h - 3))
                    s = tmp_free[0] = PL.op(lambda e: e.tensor_tensor(dst, dst, tmp, ALU.add), a, u0, u1,
                                            last_pool())
                    if not which:
                        q1t = PL.op(lambda e: e.tensor_scalar(q1, q0, mask1, None, ALU.mult), s, t_mask)
                        s = PL.op(lambda e: e.tensor_scalar(q0, q0, mask0, None, ALU.mult), q1t)
                    qk_ready.setdefault(h, []).append(s)
                return post

            a_ready, tr_done, at_ready, exp_done = {}, {}, {}, {}

            def scores(h, i):
                q0, q1, k = qk[h % 3]
                n = (i + 1) * 128
                c = (h * 4 + i) * 8
                mx, nb = stat[:, c:c + 2], stat[:, c + 2:c + 4]
                ls, r = stat[:, c + 4:c + 6], stat[:, c + 6:c + 8]
                buf = (h * 4 + i) % 2
                maxes, banks = [], []
                for m, q in enumerate((q0, q1)):
                    b = bank()
                    banks.append(b)
                    t = PE.op(lambda e, q=q, b=b: e.matmul(ps[b][:, 0:n], q[:, i * 128:i * 128 + 128], k[:, 0:n],
                                                           start=True, stop=True), qk_ready[h], rest[b])
                    qk_free[h] = t
                    t = DV.op(lambda e, b=b: e.memset(ps[b][0:64, n - 64:n], NEG), t)
                    maxes.append(DV.op(lambda e, b=b, m=m: e.reduce_max(mx[:, m:m + 1], ps[b][:, 0:n], AX), t))
                t = DV.op(lambda e: e.tensor_scalar(nb, mx, -0.125, None, ALU.mult), maxes)
                exps = []
                for m in range(2):
                    b = banks[m]
                    exps.append(AC.op(lambda e, m=m, b=b: e.activation(
                        ebuf[buf][m][:, 0:n], ps[b][:, 0:n], ACT.Exp, bias=nb[:, m:m + 1], scale=0.125,
                        accum_out=ls[:, m:m + 1]), t, tr_done.get((h * 4 + i) - 2)))
                    rest[b] = exps[-1]
                exp_done[h, i] = exps

            def shares(h, i):
                n = (i + 1) * 128
                c = (h * 4 + i) * 8
                ls, r = stat[:, c + 4:c + 6], stat[:, c + 6:c + 8]
                buf = (h * 4 + i) % 2
                t = DV.op(lambda e: e.reciprocal(r, ls), exp_done[h, i])
                r1 = DV.op(lambda e: e.tensor_tensor(r[:, 1:2], r[:, 1:2], nlam, ALU.mult), t, t_nlam)
                e0, e1 = ebuf[buf][0][:, 0:n], ebuf[buf][1][:, 0:n]
                t = DV.op(lambda e: e.tensor_scalar(e0, e0, r[:, 0:1], None, ALU.mult), t)
                a_ready[h, i] = DV.op(lambda e: e.scalar_tensor_tensor(e0, e1, r[:, 1:2], e0, ALU.mult, ALU.add), t, r1)

            def turn_over(h, i):
                buf = (h * 4 + i) % 2
                e0 = ebuf[buf][0]
                b = bank()

                def issue(e):
                    for j in range(i + 1):
                        m = e.transpose(ps[b][:, j * 128:j * 128 + 128], e0[:, j * 128:j * 128 + 128], ident[:])
                    return m
                t = PE.op(issue, a_ready[h, i], rest[b])
                tr_done[h * 4 + i] = t
                n = (i + 1) * 128
                a = AC.op(lambda e: e.activation(aT[:, 0:i + 1, i * 128:i * 128 + 128],
                                                 ps[b][:, 0:n].rearrange("p (j q) -> p j q", j=i + 1), ACT.Copy), t)
                rest[b] = a
                at_ready[h, i] = a

            sq_free = [None]

            def weigh(h):
                b = bank(hold=True)

                def issue(e):
                    for j in range(4):
                        m = e.matmul(ps[b][:, j * 128:512], V[:, j, h * 128:h * 128 + 128], aT[:, j, j * 128:512],
                                     start=(j == 0), stop=(j == 3))
                    return m
                t = PE.op(issue, v_ready, rest[b], [at_ready[h, i] for i in range(4)])
                st[h] = (b, AC.op(lambda e: e.activation(sq, ps[b][:], ACT.Square), t, l1, l2, sq_free[0]))

            st = {}

            def norm(h):
                b, t = st[h]
                b2 = bank()
                m = PE.op(lambda e: e.matmul(ps[b2][:], ones[:], sq, start=True, stop=True), t, rest[b2], t_ones)
                a = AC.op(lambda e: e.activation(sq, ps[b2][:], ACT.Ln, bias=eps5, scale=1.0 / 128), m, t_eps5)
                rest[b2] = a
                a = AC.op(lambda e: e.activation(sq, sq, ACT.Exp, scale=-0.5), a)
                o = DV.op(lambda e: e.scalar_tensor_tensor(of, ps[b][:], g8, sq, ALU.mult, ALU.mult), a, t_g8,
                          h_ready[h - 1] if h else None)
                let_go(b, o)
                sq_free[0] = o
                hi = AC.op(lambda e: e.activation(hh[:, h, :], of, ACT.Copy), o)
                lo = DV.op(lambda e: e.tensor_tensor(hl[:, h, :], of, f32(hh[:, h, :]), ALU.subtract), hi)
                h_ready[h] = [hi, lo]

            def proj(h):
                return project(rope(h, 0)) + project(rope(h, 1))

            run_all(proj(0))
            fill = [f for h in range(1, 8) for f in proj(h)] + then[:12]
            run_all(fill[:AHEAD_A])
            fill = iter(fill[AHEAD_A:])
            steps = {"S": scores, "F": shares, "T": turn_over}
            for h in range(9):
                if h < 8:
                    bias_skewed(2 * h, 2, t_rows)
                for step in ORDER_A:
                    if step == "-":
                        f = next(fill, None)
                        if f:
                            f()
                        continue
                    g = h - step[0].islower()
                    if not 0 <= g < 8:
                        continue
                    if step == "w":
                        weigh(g)
                    elif step == "n":
                        norm(g)
                    else:
                        steps[step[0].upper()](g, int(step[1]))
            run_all(fill)

        def ffn(layer, after_row, tail):
            sbuf_ = [ar(BASE + i * 512, 512) for i in range(2)]
            hbuf = [ar(BASE + 1024 + i * 512, 512) for i in range(2)]
            s_free, n = {}, [0]
            for gi, (f0, nf) in enumerate(groups):
                posts = []
                for f in range(nf):
                    st = {}

                    def post_gate(b, t, st=st):
                        i = n[0] % 2
                        st["s"] = AC.op(lambda e: e.activation(sbuf_[i], ps[b][:], ACT.Silu), t, s_free.get(n[0] - 2))
                        rest[b] = st["s"]

                    def post_up(b, t, st=st, f=f):
                        i = n[0] % 2
                        o = DV.op(lambda e: e.tensor_tensor(hbuf[i], ps[b][:], sbuf_[i], ALU.mult), t, st["s"],
                                  s_free.get(n[0] - 2))
                        rest[b] = o
                        hi = AC.op(lambda e: e.activation(hh[:, f, :], hbuf[i], ACT.Copy), o)
                        lo = DV.op(lambda e: e.tensor_tensor(hl[:, f, :], hbuf[i], f32(hh[:, f, :]), ALU.subtract), hi)
                        h_ready[f] = [hi, lo]
                        s_free[n[0]] = lo
                        n[0] += 1
                    posts += [post_gate, post_up]
                if gi:
                    AC.wait(prev)
                    DV.wait(prev)
                    run_all([piece for post in posts for piece in project(post)])
                else:
                    run_all(projections(posts, "silu_and_others"))
                last = gi == len(groups) - 1
                if last:
                    after = tail(after_row)
                post = residual_norm(last, gi == 0, after if last else None)
                run_all(tokens_out(post, hh, hl, lambda k, t: h_ready[k], nf, ends=last, pairs=last))
                prev = W.done_t[W.taken - 1]

        after = norm_then_features(0)
        pieces = tokens_out(residual_norm(True, True, after), hh, hl, lambda k, t: h_ready[k], 8, ends=True)
        attention_a(pieces)
        run_all(pieces[12:])
        ffn(0, 1, norm_then_features)

        AHEAD_B = 4
        ORDER_B = ("t13 - S00 S01 F00 w S02 F01 T00 - S03 F02 T01 - S10 F03 T02 S11 - "
                   "F10 T03 - F11 S12 T10 - S13 F12 T11 - F13 - T12").split()

        def attention_b(then):
            qk = [[ar(BASE + (n * 2 + i) * 512, 512) for i in range(2)] for n in range(2)]
            qk.append([ar(BASE + 12288 + i * 512, 512) for i in range(2)])
            V = ar(BASE + 4096, 4096).rearrange("p (t c) -> p t c", t=4)
            ebuf = [ar(BASE + 8192 + n * 512, 512) for n in range(3)]
            PT = [ar(BASE + c, 2048).rearrange("p (j q) -> p j q", j=4) for c in (10240, 13312)]
            bt = [ar(BASE + 2048 + n * 512, 512) for n in range(3)]
            v_ready, pieces = values_out(V)
            run_all(pieces)
            qk_ready, qk_free = {}, {}
            bt_ready, bt_free = {}, {}

            def load_bias(h):
                i = h % 3
                src = bass.AP(tensor=toep.tensor, offset=h * 128 * ELEN + 127, ap=[[ELEN - 1, 128], [1, 512]])
                t = SP.dma(c_b[3 + i] if i < 2 else c_b[0], bt[i], src, t_toep[-1], bt_free.get(h - 3), v_ready)
                bt_ready[h] = PL.op(lambda e: e.memset(bt[i][0:64, 448:512], NEG), t, last_pool())

            def keep(p, which):
                def post(b, t):
                    if which:
                        s = AC.op(lambda e: e.activation(qk[p % 3][1], ps[b][:], ACT.Copy), t, qk_free.get(p - 3))
                    else:
                        s = AC.op(lambda e: e.activation(qk[p % 3][0], ps[b][:], ACT.Copy, scale=0.125), t,
                                  qk_free.get(p - 3))
                    rest[b] = s
                    qk_ready.setdefault(p, []).append(s)
                return post

            p_ready, tr_done, pt_ready, exp_done = {}, {}, {}, {}

            def scores(h, i):
                p, a = divmod(h, 2)
                q, k = qk[p % 3]
                n = (i + 1) * 128
                c = (h * 4 + i) * 4
                mx, nb, ls = (stat[:, c + z:c + z + 1] for z in range(3))
                s = h * 4 + i
                e_ = ebuf[s % 3][:, 0:n]
                rows = slice(64 * a, 64 * a + 64)
                b = bank()
                t = PE.op(lambda e: e.matmul(ps[b][:, 0:n], q[rows, i * 128:i * 128 + 128], k[rows, 0:n],
                                             start=True, stop=True), qk_ready[p], rest[b])
                qk_free[p] = t
                t = DV.op(lambda e: e.tensor_tensor_reduce(e_, ps[b][:, 0:n], bt[h % 3][:, 384 - 128 * i:512], 1.0, NEG,
                                                           ALU.add, ALU.max, mx), t, bt_ready[h], tr_done.get(s - 3))
                rest[b] = t
                bt_free[h] = t
                t = DV.op(lambda e: e.tensor_scalar(nb, mx, -1.0, None, ALU.mult), t)
                exp_done[s] = AC.op(lambda e: e.activation(e_, e_, ACT.Exp, bias=nb, accum_out=ls), t)

            def shares(h, i):
                c = (h * 4 + i) * 4
                ls, r = stat[:, c + 2:c + 3], stat[:, c + 3:c + 4]
                s = h * 4 + i
                e_ = ebuf[s % 3][:, 0:(i + 1) * 128]
                t = DV.op(lambda e: e.reciprocal(r, ls), exp_done[s])
                p_ready[s] = DV.op(lambda e: e.tensor_scalar(e_, e_, r, None, ALU.mult), t)

            def turn_over(h, i):
                s = h * 4 + i
                e_ = ebuf[s % 3]
                b = bank()

                def issue(e):
                    for j in range(i + 1):
                        m = e.transpose(ps[b][:, j * 128:j * 128 + 128], e_[:, j * 128:j * 128 + 128], ident[:])
                    return m
                t = PE.op(issue, p_ready[s], rest[b])
                tr_done[s] = t
                n = (i + 1) * 128
                pt_ready[h, i] = rest[b] = AC.op(lambda e: e.activation(
                    PT[h % 2][:, 0:i + 1, i * 128:i * 128 + 128],
                    ps[b][:, 0:n].rearrange("p (j q) -> p j q", j=i + 1), ACT.Copy), t)

            def weigh(p):
                b = bank(hold=True)

                def issue(e):
                    for j in range(4):
                        for a in range(2):
                            h = 2 * p + a
                            m = e.matmul(ps[b][64 * a:64 * a + 64, j * 128:512], V[:, j, h * 64:h * 64 + 64],
                                         PT[a][:, j, j * 128:512], start=(j == 0), stop=(j == 3))
                    return m
                t = PE.op(issue, v_ready, rest[b], [pt_ready[2 * p + a, i] for a in range(2) for i in range(4)])
                hi = AC.op(lambda e: e.activation(hh[:, p, :], ps[b][:], ACT.Copy), t)
                lo = DV.op(lambda e: e.tensor_tensor(hl[:, p, :], ps[b][:], f32(hh[:, p, :]), ALU.subtract), hi)
                let_go(b, lo)
                h_ready[p] = [hi, lo]

            def proj(p):
                return project(keep(p, 0)) + project(keep(p, 1))

            load_bias(0)
            load_bias(1)
            run_all(proj(0))
            fill = [f for p in range(1, 8) for f in proj(p)] + then[:12]
            run_all(fill[:AHEAD_B])
            fill = iter(fill[AHEAD_B:])
            steps = {"S": scores, "F": shares, "T": turn_over}
            for p in range(9):
                for step in ORDER_B:
                    if step == "-":
                        f = next(fill, None)
                        if f:
                            f()
                        continue
                    g = p - step[0].islower()
                    if not 0 <= g < 8:
                        continue
                    if step == "w":
                        weigh(g)
                        continue
                    h, i = 2 * g + int(step[1]), int(step[2])
                    if step[0] == "S" and i == 2 and h + 2 < 16:
                        load_bias(h + 2)
                    steps[step[0].upper()](h, i)
            run_all(fill)

        after = norm_then_features(2)
        pieces = tokens_out(residual_norm(True, True, after), hh, hl, lambda k, t: h_ready[k], 8, ends=True)
        attention_b(pieces)
        run_all(pieces[12:])

        yb = [ar(9216 + i * 1024, 1024) for i in range(2)]
        y_free = [None, None]

        def rms_features(t, tg, ready):
            y = yb[t % 2]
            done = []

            def scale():
                a = AC.op(lambda e: e.activation(y, x[:, t, :], ACT.Square, accum_out=lsum[:, t:t + 1]), ready,
                          y_free[t % 2])
                a = AC.op(lambda e: e.activation(lsum[:, 4 + t:5 + t], lsum[:, t:t + 1], ACT.Sqrt, bias=eps6,
                                                 scale=1.0 / D), a, t_eps6)
                r = DV.op(lambda e: e.reciprocal(rs[:, t:t + 1], lsum[:, 4 + t:5 + t]), a)
                for half in range(2):
                    c = slice(half * 512, half * 512 + 512)
                    done.append(DV.op(lambda e, c=c: e.scalar_tensor_tensor(y[:, c], x[:, t, c], rs[:, t:t + 1],
                                                                            gvec[2][:, c], ALU.mult, ALU.mult),
                                      r, tg, y_free[t % 2]))
                last_g[2] = done
            waiting.append(scale)

            def pe():
                to_features(t, y, done)
                y_free[t % 2] = (PE.count, PE.count.value)
            return pe

        def tail_two(row):
            l, r_ = divmod(row, 2)
            tg = load_g(0, ap["ln_g"][l, r_], last_g[0])
            tb = load_g(1, ap["ln_b"][l, r_], last_g[1])
            tp = load_g(2, ap["pre_mix_g_2"][0], last_g[2])

            def after(t, m):
                a = layer_norm(t, m, tg, tb)
                last_g[0] = last_g[1] = a
                return rms_features(t, tp, a)
            return after
        ffn(1, 3, tail_two)

        def mixer():
            v = ar(3072, 2048).rearrange("p (t c) -> p t c", t=4)
            vb = ar(5120, 2048).rearrange("p (t c) -> p t c", t=4)
            qe = [ar(7168 + p * 512, 512) for p in range(2)]
            ke = [ar(8192 + p * 512, 512) for p in range(2)]
            outa = ar(7168, 2048).rearrange("p (h q) -> p h q", h=4)
            la = ar(9216, 1024).rearrange("p (t c) -> p t c", t=4)
            cum = [ar(10240, 512), ar(10752, 512)]
            on = ar(9216, 2048).rearrange("p (h q) -> p h q", h=4)
            ex = [ar(11264, 512), ar(11776, 512)]
            sc = [ar(12288 + i * 512, 512).rearrange("p (t c) -> p t c", t=4) for i in range(2)]
            wT = ar(13312, 512).rearrange("p (h i) -> p h i", h=4)
            sq, rinv, of, ub = (ar(13824 + i * 512, 512) for i in range(4))
            wsb = ar(15872, 512).rearrange("p (h j) -> p h j", h=4)
            bsr = ar(16384, 512)
            gw, gb = ar(16896, 256), ar(17152, 512)
            zl = ar(17664, 512)
            lng, lnb = ar(18176, 512), ar(18688, 512)
            kd = [ar(p * 512, 512).rearrange("p (t c) -> p t c", t=4) for p in range(2)]
            St = ar(1024, 1792).rearrange("p (n c) -> p n c", n=14)
            tri = sb("tri", [128, 128])
            t_tri = SP.dma(c_in[5], tri[:], ap["c_tri"])
            wide = lambda u, n: bass.AP(tensor=u.tensor, offset=u.offset, ap=[[0, 128], [1, n]])
            SP.wait(x_tile[0])
            t_ws = SP.dma(c_in[6], wsb, ap["gmlp_ws_2"][0].rearrange("h i j -> i h j"))
            SP.dma(c_in[7], bsr[0:1, :], ap["gmlp_bs_2"].rearrange("a h i -> a (h i)"))
            SP.dma(c_in[7], gw[0:16, :], ap["gla_gate_w_2"][0])
            SP.dma(c_in[7], gb[0:1, 0:256], ap["gla_gate_b_2"])
            SP.dma(c_in[7], gb[0:1, 256:512], ap["gla_gate_b_2"])
            SP.dma(c_in[7], gocol, ap["gmlp_out_g_2"][0].rearrange("(h p) -> p h", p=128), slow=True)
            t_sm = SP.dma(c_in[7], blcol, ap["gla_out_g_2"][0].rearrange("(h p) -> p h", p=128), slow=True)
            SP.dma(c_in[8], lng, wide(ap["gmlp_ln_g_2"][0], 512))
            t_ln = SP.dma(c_in[8], lnb, wide(ap["gmlp_ln_b_2"][0], 512))

            tk = {}

            def post_zlr(b, t):
                tk["zl"] = rest[b] = AC.op(lambda e: e.activation(zl[0:16, :], ps[b][0:16, :], ACT.Copy), t)

            def keep(dst, name, scale=1.0):
                def post(b, t):
                    tk[name] = rest[b] = AC.op(lambda e: e.activation(dst, ps[b][:], ACT.Copy, scale=scale), t)
                return post

            def gate():
                for half in range(2):
                    b = bank()

                    def issue(e, half=half, b=b):
                        e.matmul(ps[b][:], ones[0:1, :], gb[0:1, :], start=True, stop=True,
                                 skip_group_check=True)
                        for i in range(2):
                            t = half * 2 + i
                            m = e.matmul(ps[b][:, i * 256:i * 256 + 256], zl[0:16, t * 128:t * 128 + 128], gw[0:16, :],
                                         start=False, stop=True, skip_group_check=True)
                        return m
                    t = PE.op(issue, tk["zl"], t_sm, rest[b], t_ones)
                    low = la[:, 2 * half:2 * half + 2, :].rearrange("p t c -> p (t c)")
                    ln = ex[half]
                    a = AC.op(lambda e, b=b, ln=ln: e.activation(ln, ps[b][:], ACT.Abs), t)
                    m = DV.op(lambda e, b=b, low=low: e.tensor_scalar(low, ps[b][:], 0.0, None, ALU.min), a)
                    rest[b] = m
                    a = AC.op(lambda e, ln=ln: e.activation(ln, ln, ACT.Exp, scale=-1.0), a)
                    a = AC.op(lambda e, ln=ln: e.activation(ln, ln, ACT.Ln, bias=1.0), a)
                    tk["la", half] = DV.op(lambda e, ln=ln, low=low: e.tensor_tensor(low, low, ln, ALU.subtract), m, a)

            def cumulate(p):
                b = bank()

                def issue(e):
                    for t in range(4):
                        m = e.matmul(ps[b][:, t * 128:t * 128 + 128], la[:, t, p * 128:p * 128 + 128], tri[:],
                                     start=True, stop=True)
                    return m
                t = PE.op(issue, tk["la", 0], tk["la", 1], t_tri, rest[b])
                tk["cum", p] = rest[b] = DV.op(lambda e: e.tensor_copy(cum[p], ps[b][:]), t)

            def decays(p):
                c3 = cum[p].rearrange("p (n i) -> p n i", n=8)
                x0, x1 = ex
                a = AC.op(lambda e: e.activation(x0, cum[p], ACT.Exp), tk["cum", p], tk["la", 0], tk["la", 1], tk.get("ex0"))
                d = DV.op(lambda e: e.tensor_copy(dec[:, p * 8:p * 8 + 8],
                                                  x0.rearrange("p (n i) -> p n i", n=8)[:, :, 63]), a)
                q = DV.op(lambda e: e.tensor_tensor(qe[p], qe[p], x0, ALU.mult), a, tk["q", p])
                tk["dec", p], tk["qe", p] = d, q
                l = DV.op(lambda e: e.tensor_tensor(x1.rearrange("p (n i) -> p n i", n=8),
                                                    c3[:, :, 63:64].broadcast_to([128, 8, 64]), c3, ALU.subtract),
                          tk["cum", p], tk["la", 0], tk["la", 1], tk.get("ex1"))
                l = AC.op(lambda e: e.activation(x1, x1, ACT.Exp), l)
                l = DV.op(lambda e: e.tensor_tensor(x1, x1, ke[p], ALU.mult), l, tk["k", p])
                tk["kdT", p] = l
                a = AC.op(lambda e: e.activation(x0, cum[p], ACT.Exp, scale=-1.0), d, q)
                tk["ke", p] = tk["ex0"] = DV.op(lambda e: e.tensor_tensor(ke[p], ke[p], x0, ALU.mult), a, l)

            def turn_kd(p):
                x1 = ex[1]
                b = bank()

                def issue(e):
                    for t in range(4):
                        m = e.transpose(ps[b][:, t * 128:t * 128 + 128], x1[:, t * 128:t * 128 + 128], ident[:])
                    return m
                t = PE.op(issue, tk["kdT", p], rest[b])
                tk["ex1"] = t
                tk["kd", p] = rest[b] = AC.op(lambda e: e.activation(
                    kd[p], ps[b][:].rearrange("p (t c) -> p t c", t=4), ACT.Copy), t)

            def updates(p):
                banks, made = [], []
                for odd in range(2):
                    rows = slice(64 * odd, 64 * odd + 64)
                    b = bank()

                    def issue(e, odd=odd, rows=rows, b=b):
                        for n in range(odd, 7, 2):
                            for a in range(2):
                                c = (n // 2) * 128
                                m = e.matmul(ps[b][64 * a:64 * a + 64, c:c + 128],
                                             kd[p][rows, n // 2, a * 64:a * 64 + 64],
                                             vb[rows, n // 2, (2 * p + a) * 128:(2 * p + a) * 128 + 128],
                                             start=True, stop=True)
                        return m
                    banks.append(b)
                    made.append(PE.op(issue, tk["kd", p], tk["vb"], rest[b]))
                for n in range(7):
                    c = (n // 2) * 128
                    u = ps[banks[n % 2]][:, c:c + 128]
                    s = p * 7 + n
                    if n == 0:
                        a = DV.op(lambda e, u=u, s=s: e.tensor_copy(St[:, s, :], u), made)
                    else:
                        a = DV.op(lambda e, u=u, s=s, n=n: e.scalar_tensor_tensor(
                            St[:, s, :], St[:, s - 1, :], dec[:, p * 8 + n:p * 8 + n + 1], u,
                            ALU.mult, ALU.add), a, tk["dec", p])
                    rest[banks[n % 2]] = a
                tk["S", p] = a

            def inner(h):
                p, a = divmod(h, 2)
                rows = slice(64 * a, 64 * a + 64)
                b = bank()

                def issue(e):
                    for t in range(4):
                        c = slice(t * 128, t * 128 + 128)
                        m = e.matmul(ps[b][:, c], ke[p][rows, c], qe[p][rows, c], start=True, stop=True)
                    return m
                t = PE.op(issue, tk["ke", p], tk["qe", p], rest[b])
                s_ = sc[h % 2]
                a_ = AC.op(lambda e: e.activation(s_, ps[b][:].rearrange("p (t c) -> p t c", t=4), ACT.Copy), t,
                           tk.get(("o", h - 2)))
                rest[b] = a_
                m = PL.op(lambda e: e.affine_select(out=s_, in_=s_, compare_op=ALU.is_ge, fill=0.0, base=0,
                                                    pattern=[[0, 4], [1, 128]], channel_multiplier=-1), a_, last_pool())
                tk["sc", h] = PL.op(lambda e: e.memset(s_[0:64, :, 64:128], 0.0), m, last_pool())

            def outer(h):
                p, a = divmod(h, 2)
                rows = slice(64 * a, 64 * a + 64)
                b = bank(hold=True)
                s_ = sc[h % 2]

                def issue(e):
                    for t in range(4):
                        m = e.matmul(ps[b][:, t * 128:t * 128 + 128], vb[:, t, h * 128:h * 128 + 128], s_[:, t, :],
                                     start=(t == 0), stop=(t == 3), skip_group_check=True)
                        for n in (2 * t, 2 * t + 1):
                            if n:
                                m = e.matmul(ps[b][:, n * 64:n * 64 + 64], St[rows, p * 7 + n - 1, :],
                                             qe[p][rows, n * 64:n * 64 + 64], start=False, stop=(n == 7),
                                             skip_group_check=True)
                    return m
                t = PE.op(issue, tk["sc", h], tk["vb"], tk["S", p], rest[b])
                tk["o", h] = t
                tk["sq"] = AC.op(lambda e: e.activation(sq, ps[b][:], ACT.Square), t, tk.get("sq_free"))
                tk["ob", h] = b

            def outer_norm(h):
                b = tk["ob", h]
                b2 = bank()
                m = PE.op(lambda e: e.matmul(ps[b2][:], ones[:], sq, start=True, stop=True), tk["sq"], rest[b2])
                table("natural_log_exp_and_others")
                a = AC.op(lambda e: e.activation(rinv, ps[b2][:], ACT.Ln, bias=eps6, scale=1.0 / 128), m, t_eps6,
                          tk.get("rinv_free"))
                rest[b2] = a
                a = AC.op(lambda e: e.activation(rinv, rinv, ACT.Exp, scale=-0.5), a)
                tk["sq_free"] = a
                tk["on", h] = DV.op(lambda e: e.scalar_tensor_tensor(
                    on[:, h, :], ps[b][:], blcol[:, h:h + 1], rinv, ALU.mult, ALU.mult), a, t_sm)
                tk["rinv_free"] = tk["on", h]
                let_go(b, tk["on", h])

            def post_zg(h):
                def post(b, t):
                    s = AC.op(lambda e: e.activation(ub, ps[b][:], ACT.Silu), t, tk.get("ub_free"))
                    rest[b] = s
                    o = DV.op(lambda e: e.tensor_tensor(of, ub, on[:, h, :], ALU.mult), s, tk["on", h],
                              tk.get("of_free"))
                    tk["ub_free"] = o
                    hi = AC.op(lambda e: e.activation(hh[:, 4 + h, :], of, ACT.Copy), o)
                    lo = DV.op(lambda e: e.tensor_tensor(hl[:, 4 + h, :], of, f32(hh[:, 4 + h, :]), ALU.subtract), hi)
                    tk["of_free"] = lo
                    h_ready[4 + h] = [hi, lo]
                return post

            def rows_half(name, dst, act, extra=None):
                banks = {}

                def piece(kb):
                    if kb == 0:
                        for t in range(4):
                            banks[t] = bank(hold=True)
                    j, wh, wl, ready = W.take()
                    for t in range(4):
                        def issue(e, t=t):
                            for k in (0, 1):
                                a = slice(t * 128, t * 128 + 128)
                                m = mm3(e, ps[banks[t]][:], xh[:, 2 * kb + k, a], xl[:, 2 * kb + k, a],
                                        wh[:, k, :], wl[:, k, :], kb + k == 0, 2 * kb + k == 7)
                            return m
                        need = [ready, rest[banks[t]] if kb == 0 else None, x_tile]
                        if kb == 3 or t == 3:
                            tok = PE.op(issue, need)
                        else:
                            PE.quiet(issue, need)
                        if t == 3:
                            W.done(j, tok)
                        if kb == 3:
                            b = banks[t]
                            s = AC.op(lambda e, b=b, t=t: e.activation(dst[:, t, :], ps[b][:], act), tok)
                            let_go(b, s)
                            if extra:
                                s = extra(t, s)
                            tk.setdefault(name, []).append(s)
                return [lambda kb=kb: piece(kb) for kb in range(4)]

            def v_moments(t, ready):
                m = moments(t, 0, v[:, t, :], ready)
                return DV.op(lambda e: e.bn_aggr(mv[:, 2 * t:2 * t + 2], bst[:, t * 12:t * 12 + 6]), m)

            def v_norm():
                a = AC.op(lambda e: e.activation(lsum[:, 0:4], mv.rearrange("p (t c) -> p t c", t=4)[:, :, 1],
                                                 ACT.Sqrt, bias=eps6), tk["v"], t_eps6)
                r = DV.op(lambda e: e.reciprocal(rs[:, 0:4], lsum[:, 0:4]), a)
                done = []
                for t in range(4):
                    a = DV.op(lambda e, t=t: e.scalar_tensor_tensor(v[:, t, :], v[:, t, :], mv[:, 2 * t:2 * t + 1],
                                                                    lng, ALU.subtract, ALU.mult), r, t_ln)
                    done.append(DV.op(lambda e, t=t: e.scalar_tensor_tensor(v[:, t, :], v[:, t, :], rs[:, t:t + 1],
                                                                            lnb, ALU.mult, ALU.add), a))
                tk["v"] = done

            def turn_ws():
                b = bank()

                def issue(e):
                    for h in range(4):
                        m = e.transpose(ps[b][:, h * 128:h * 128 + 128], wsb[:, h, :], ident[:])
                    return m
                t = PE.op(issue, t_ws, rest[b])
                a = rest[b] = AC.op(lambda e: e.activation(wT, ps[b][:].rearrange("p (t c) -> p t c", t=4), ACT.Copy), t)
                tk["wT"] = PL.op(lambda e: e.memset(wT[64:128, :, 0:64], 0.0), a, last_pool())

            def mixed(h):
                b = bank()

                def issue(e):
                    e.matmul(ps[b][:].rearrange("p (n i) -> p n i", n=4), ones[0:1, :],
                             bsr[0:1, h * 128:h * 128 + 128].unsqueeze(1).broadcast_to([1, 4, 128]),
                             start=True, stop=True, skip_group_check=True)
                    for t in range(4):
                        m = e.matmul(ps[b][:, t * 128:t * 128 + 128], v[:, t, h * 128:h * 128 + 128], wT[:, h, :],
                                     start=False, stop=True, skip_group_check=True)
                    return m
                tk["mx", h] = (b, PE.op(issue, tk["v"], tk["wT"], t_sm, rest[b]))

            def post_zu(h):
                def post(b, t):
                    s = AC.op(lambda e: e.activation(ub, ps[b][:], ACT.Gelu_apprx_tanh), t, tk.get("ub_free"))
                    rest[b] = s
                    mixed(h)
                    mb, mt = tk["mx", h]
                    o = DV.op(lambda e: e.tensor_tensor(outa[:, h, :], ps[mb][:], ub, ALU.mult), s, mt,
                              tk["o", 3], tk.get("ub_free"))
                    rest[mb] = o
                    tk["ub_free"] = o
                    q = AC.op(lambda e: e.activation([sq, of][h % 2], outa[:, h, :], ACT.Square), o,
                              tk.get(("sqm", h - 2)), tk.get("of_free"), tk.get("sq_free"))
                    tk["sqr", h] = q
                return post

            def squares(h):
                if h == 0:
                    tk["rb"] = bank(hold=True)
                rb = tk["rb"]
                tk["sqm", h] = PE.op(lambda e: e.matmul(ps[rb][:], ones[:], [sq, of][h % 2], start=(h == 0),
                                                        stop=(h == 3)), tk["sqr", h], rest[rb] if h == 0 else None)

            run_all(projections([post_zlr, keep(ke[0], ("k", 0)), keep(ke[1], ("k", 1))], "natural_log_exp_and_others"))
            pq = [project(keep(qe[p], ("q", p), 0.125)) for p in range(2)]
            gate()
            turn_ws()
            for f in pq[0]:
                f()
            cumulate(0)
            cumulate(1)
            run_all(pq[1])
            decays(0)
            pb = rows_half("vb", vb, ACT.Copy)
            pb[0]()
            turn_kd(0)
            decays(1)
            pb[1]()
            turn_kd(1)
            run_all(pb[2:])
            pv = rows_half("v", v, ACT.Gelu_apprx_tanh, v_moments)
            pv[0]()
            inner(0)
            inner(1)
            updates(0)
            pv[1]()
            updates(1)
            pv[2]()
            outer(0)
            pv[3]()
            v_norm()
            table("natural_log_exp_and_others")
            fill = []
            for h in range(4):
                fill += project(post_zg(h))
            order = [lambda: outer_norm(0), lambda: inner(2), lambda: outer(1), lambda: outer_norm(1),
                     lambda: inner(3), lambda: outer(2), lambda: outer_norm(2), lambda: outer(3),
                     lambda: outer_norm(3)]
            at = [0, 0, 2, 5, 5, 7, 10, 11, 14]
            for i, f in enumerate(fill):
                for n, o in zip(at, order):
                    if n == i:
                        o()
                f()
            for h in range(4):
                pieces = project(post_zu(h))
                if h:
                    pieces[3:3] = [lambda h=h: squares(h - 1)]
                run_all(pieces)
            pieces = w_out()
            run_all(pieces[:2])
            squares(3)
            rb = tk["rb"]
            table("natural_log_exp_and_others")
            a = AC.op(lambda e: e.activation(rinv, ps[rb][:], ACT.Ln, bias=eps6, scale=1.0 / 512), tk["sqm", 3],
                      tk["rinv_free"])
            let_go(rb, a)
            a = AC.op(lambda e: e.activation(rinv, rinv, ACT.Exp, scale=-0.5), a)
            for h in range(4):
                o = DV.op(lambda e, h=h: e.scalar_tensor_tensor(outa[:, h, :], outa[:, h, :], gocol[:, h:h + 1], rinv,
                                                                ALU.mult, ALU.mult), a)
                hi = AC.op(lambda e, h=h: e.activation(hh[:, h, :], outa[:, h, :], ACT.Copy), o)
                lo = DV.op(lambda e, h=h: e.tensor_tensor(hl[:, h, :], outa[:, h, :], f32(hh[:, h, :]), ALU.subtract), hi)
                h_ready[h] = [hi, lo]
            return pieces[2:]

        mb = ar(3072, 4096).rearrange("p (t c) -> p t c", t=4)
        tw = {}

        def add_rms(t, m, tg):
            return add_scaled(t, inv_std(t, 2, eps6, t_eps6, False, m), tg, DV)

        def add_scaled(t, r, tg, second):
            done, used = [], []
            for half in range(2):
                c = slice(half * 512, half * 512 + 512)
                a = DV.op(lambda e, c=c: e.scalar_tensor_tensor(mb[:, t, c], mb[:, t, c], rs[:, t:t + 1],
                                                                gvec[0][:, c], ALU.mult, ALU.mult), r, tg)
                used.append(a)
                q = second if half else DV
                done.append(q.op(lambda e, c=c: e.tensor_tensor(x[:, t, c], x[:, t, c], mb[:, t, c], ALU.add), a,
                                 last_pool() if q is PL else None))
            last_g[0] = used
            return done

        def post_w(nh, t, b, token):
            cols = slice(nh * 512, nh * 512 + 512)
            a = rest[b] = AC.op(lambda e: e.activation(mb[:, t, cols], ps[b][:], ACT.Copy), token)
            m = moments(t, nh, mb[:, t, cols], a)
            if nh == 0:
                return None
            return rms_features(t, tw["pre"], add_rms(t, m, tw["post"]))

        def w_out():
            tw["post"] = load_g(0, ap["post_mix_g_2"][0], h_ready[7])
            tw["pre"] = load_g(2, ap["pre_ff_g_2"][0], h_ready[7])
            return tokens_out(post_w, hh, hl, lambda k, t: h_ready[k], 8, 4, ends=True, pairs=True)

        run_all(mixer())


        rbuf = [ar(7168 + i * 512, 512) for i in range(2)]
        fbuf = [ar(8192 + i * 512, 512) for i in range(2)]
        junk, sums = ar(9216, 512), small[:, 104:112]
        squared, sum_of = [None], {}
        free, n = {}, [0]
        tg = load_g(0, ap["post_ff_g_2"][0], last_g[0])
        c_out = count("s_out")
        prev = None
        for g in range(4):
            posts = []
            for f in range(8):
                def post(b, t, f=f):
                    i = n[0] % 2
                    s = AC.op(lambda e: e.activation(rbuf[i], ps[b][:], ACT.Relu), t, free.get(n[0] - 2))
                    o = DV.op(lambda e: e.tensor_tensor(fbuf[i], rbuf[i], ps[b][:], ALU.mult), s)
                    rest[b] = o
                    hi = AC.op(lambda e: e.activation(hh[:, f, :], fbuf[i], ACT.Copy), o, prev)
                    lo = DV.op(lambda e: e.tensor_tensor(hl[:, f, :], fbuf[i], f32(hh[:, f, :]), ALU.subtract), hi, prev)
                    h_ready[f] = [hi, lo]
                    free[n[0]] = lo
                    n[0] += 1
                posts.append(post)
            run_all([piece for post in posts for piece in project(post)] if g else projections(posts, "sqrt_and_others"))

            def post_f(nh, t, b, token, g=g):
                cols = slice(nh * 512, nh * 512 + 512)
                if g == 0:
                    a = AC.op(lambda e: e.activation(mb[:, t, cols], ps[b][:], ACT.Copy), token)
                else:
                    a = DV.op(lambda e: e.tensor_tensor(mb[:, t, cols], mb[:, t, cols], ps[b][:], ALU.add), token)
                rest[b] = a
                if g < 3:
                    return None
                a = squared[0] = AC.op(lambda e: e.activation(junk, mb[:, t, cols], ACT.Square,
                                                              accum_out=sums[:, nh * 4 + t:nh * 4 + t + 1]),
                                       a, squared[0])
                sum_of[nh, t] = a
                if nh == 0:
                    return None
                total, root, r = lsum[:, t:t + 1], lsum[:, 4 + t:5 + t], rs[:, t:t + 1]
                a = DV.op(lambda e: e.tensor_tensor(total, sums[:, t:t + 1], sums[:, 4 + t:5 + t], ALU.add), a,
                          sum_of[0, t])
                a = AC.op(lambda e: e.activation(root, total, ACT.Sqrt, bias=eps6, scale=1.0 / D), a)
                a = DV.op(lambda e: e.reciprocal(r, root), a)
                a = add_scaled(t, a, tg, PL if t < 3 else DV)
                for half in range(2):
                    c = slice(half * 512, half * 512 + 512)
                    SP.dma(c_out, out[0, t * 128:(t + 1) * 128, c], x[:, t, c], a[half])
                return None
            run_all(tokens_out(post_f, hh, hl, lambda k, t: h_ready[k], 8))
            prev = W.done_t[W.taken - 1]
        SP.wait((c_out, c_out.value))
        emit(nc, ctx, PE, AC, DV, PL, SP)


def emit(nc, ctx, PE, AC, DV, PL, SP):
    block = ctx.enter_context(nc.Block())
    block.tensor(PE.play)
    block.scalar(AC.play)
    block.vector(DV.play)
    block.gpsimd(PL.play)
    block.sync(SP.play)


def constants():
    inv = (np.float32(10000.0) ** (-np.arange(0, 64, 2, dtype=np.float32) / np.float32(64))).astype(np.float32)
    ang = np.arange(S, dtype=np.float32)[:, None] * inv[None, :]
    cos, sin = np.cos(ang.astype(np.float64)), np.sin(ang.astype(np.float64))
    d = np.arange(128) % 32
    c = cos.T[d].astype(np.float32)
    s = (sin.T[d] * np.where(np.arange(128) < 64, 1.0, -1.0)[:, None]).astype(np.float32)
    m = ((np.arange(128) // 32) % 2).astype(np.float32)
    j, i = np.arange(128)[:, None], np.arange(128)[None, :]
    tri = np.where((j <= i) & (j // 64 == i // 64), np.float32(1 / 16), np.float32(0)).astype(np.float32)
    return {
        "c_ident": np.eye(128, dtype=np.float32), "c_cos": np.ascontiguousarray(c),
        "c_sin": np.ascontiguousarray(s), "c_mask": np.ascontiguousarray(np.stack([1 - m, m], 1)), "c_tri": tri,
    }


def halves_first(w):
    qk = w[..., :2 * D].reshape(D, 16, 2, 2, 32).transpose(0, 1, 3, 2, 4).reshape(1, D, 2 * D)
    return np.concatenate([qk, w[..., 2 * D:]], axis=-1)


_INS = ["x", "a_w_qkv", "a_lambda", "a_subln_g", "a_w_o", "kv_w", "b_w_q", "b_rel_bias", "b_w_o", "ln_g", "ln_b",
        "ffn_w_in", "ffn_w_out", "pre_mix_g_2", "w_in_2", "gmlp_ln_g_2", "gmlp_ln_b_2", "gmlp_ws_2", "gmlp_bs_2",
        "gmlp_out_g_2", "gla_gate_w_2", "gla_gate_b_2", "gla_out_g_2", "w_out_2", "post_mix_g_2", "pre_ff_g_2",
        "w_ff1_2", "w_ff2_2", "post_ff_g_2"]


def kernel(**inputs):
    import concourse.bacc as _bacc
    from concourse.bass_utils import run_bass_kernel_spmd as _run

    nc = _bacc.Bacc("TRN2", target_bir_lowering=False, num_devices=1)
    arrays, aps = {}, {}
    given = {name: np.ascontiguousarray(inputs[name]) for name in _INS}
    given["a_w_qkv"] = halves_first(given["a_w_qkv"])
    given.update(constants())
    for name, a in given.items():
        arrays[f"in_{name}"] = a
        aps[name] = nc.dram_tensor(f"in_{name}", a.shape, mybir.dt.from_np(a.dtype), kind="ExternalInput").ap()
    out = nc.dram_tensor("out_0", (1, S, D), F32, kind="ExternalOutput").ap()
    build(nc, aps, out)
    r = _run(nc, [arrays], core_ids=[0])
    return r.results[0]["out_0"]
```
